# Optimizing a Trainium2 kernel written in Bass

```python
import math
import jax, jax.numpy as jnp
from jax import lax
import numpy as np

D_MODEL = 2048
BATCH = 1
SEQ = 512
DEPTH = 1

CHUNK = 64
MIX_WIDTH = D_MODEL
SSM_WIDTH = MIX_WIDTH // 2
POOL_WIDTH = MIX_WIDTH - SSM_WIDTH
SSM_GROUP = 16
SSM_GROUPS = SSM_WIDTH // SSM_GROUP
SSM_STATE = 64
POOL_WINDOWS = (2, 4, 8, 16)
POOL_GROUPS = len(POOL_WINDOWS)
POOL_GROUP = POOL_WIDTH // POOL_GROUPS
D_FF = ((8 * D_MODEL // 3 + 255) // 256) * 256
EPS = 1e-6
DT_MIN = 1e-3
DT_MAX = 1e-1

kernel_name = "hybrid_s5_multiscale_pool_block"

def rms_norm(x, gain):
    xf = x.astype(jnp.float32)
    y = xf * lax.rsqrt(jnp.mean(xf * xf, axis=-1, keepdims=True) + EPS)
    return y * gain.astype(jnp.float32)

def s5_mixer(u, lam_re, lam_im, log_step, b_re, b_im, c_re, c_im, d_skip, w_glu, b_glu):
    bsz, L, _ = u.shape
    f32 = jnp.float32
    ug = u.astype(f32).reshape(bsz, L, SSM_GROUPS, SSM_GROUP)
    lam = lax.complex(lam_re.astype(f32), lam_im.astype(f32))
    step = jnp.exp(log_step.astype(f32))[:, None]
    lam_bar = jnp.exp(lam * step)
    bmat = lax.complex(b_re.astype(f32), b_im.astype(f32))
    b_bar = ((lam_bar - 1.0) / lam)[..., None] * bmat
    bu = jnp.einsum('blgh,gph->blgp', ug, b_bar)
    a = jnp.broadcast_to(lam_bar, bu.shape)

    def combine(left, right):
        a_l, b_l = left
        a_r, b_r = right
        return a_r * a_l, a_r * b_l + b_r

    _, states = lax.associative_scan(combine, (a, bu), axis=1)
    cmat = lax.complex(c_re.astype(f32), c_im.astype(f32))
    y = jnp.real(jnp.einsum('blgp,ghp->blgh', states, cmat)) + d_skip.astype(f32) * ug
    y = y.reshape(bsz, L, SSM_WIDTH)
    g = jax.nn.gelu(y, approximate=False)
    return g * jax.nn.sigmoid(g @ w_glu.astype(f32) + b_glu.astype(f32))

def pool_mixer(v, w_pool, b_pool, pool_scale):
    bsz, L, _ = v.shape
    f32 = jnp.float32
    vg = v.astype(f32).reshape(bsz, L, POOL_GROUPS, POOL_GROUP)
    cs = jnp.pad(jnp.cumsum(vg, axis=1), ((0, 0), (1, 0), (0, 0), (0, 0)))
    pos1 = jnp.arange(1, L + 1)
    outs = []
    for k, w in enumerate(POOL_WINDOWS):
        c = cs[:, :, k]
        hi = c[:, 1:]
        lo = jnp.pad(c, ((0, 0), (w, 0), (0, 0)))[:, 1:L + 1]
        count = jnp.minimum(pos1, w).astype(f32)[None, :, None]
        outs.append((hi - lo) / count - vg[:, :, k])
    pooled = jnp.stack(outs, axis=2)
    mixed = jnp.einsum('blkc,kcd->blkd', pooled, w_pool.astype(f32)) + b_pool.astype(f32)
    return mixed.reshape(bsz, L, POOL_WIDTH) * pool_scale.astype(f32)

def setup_inputs(seed: int = 0) -> dict:
    key = jax.random.key(seed)
    ks = jax.random.split(key, 24)
    f32 = jnp.float32
    nrm = lambda k, shape, s: jax.random.normal(k, shape, f32) * s
    gain = lambda k, shape: 1.0 + 0.02 * jax.random.normal(k, shape, f32)
    G, P, H = SSM_GROUPS, SSM_STATE, SSM_GROUP
    lam_im0 = jnp.pi * jnp.arange(P, dtype=f32)
    return {
        "x": jax.random.normal(ks[0], (BATCH, SEQ, D_MODEL), f32),
        "norm_mix": gain(ks[1], (DEPTH, D_MODEL)),
        "w_in": nrm(ks[2], (DEPTH, D_MODEL, MIX_WIDTH), D_MODEL ** -0.5),
        "lambda_re": -0.5 + 0.01 * jax.random.normal(ks[3], (DEPTH, G, P), f32),
        "lambda_im": lam_im0 + 0.01 * jax.random.normal(ks[4], (DEPTH, G, P), f32),
        "log_step": jax.random.uniform(ks[5], (DEPTH, G), f32, math.log(DT_MIN), math.log(DT_MAX)),
        "b_re": nrm(ks[6], (DEPTH, G, P, H), (2.0 * H) ** -0.5),
        "b_im": nrm(ks[7], (DEPTH, G, P, H), (2.0 * H) ** -0.5),
        "c_re": nrm(ks[8], (DEPTH, G, H, P), (2.0 * P) ** -0.5),
        "c_im": nrm(ks[9], (DEPTH, G, H, P), (2.0 * P) ** -0.5),
        "d_skip": nrm(ks[10], (DEPTH, G, H), 1.0),
        "w_glu": nrm(ks[11], (DEPTH, SSM_WIDTH, SSM_WIDTH), SSM_WIDTH ** -0.5),
        "b_glu": nrm(ks[12], (DEPTH, SSM_WIDTH), 0.01),
        "w_pool": nrm(ks[13], (DEPTH, POOL_GROUPS, POOL_GROUP, POOL_GROUP), POOL_GROUP ** -0.5),
        "b_pool": nrm(ks[14], (DEPTH, POOL_GROUPS, POOL_GROUP), 0.01),
        "pool_scale": gain(ks[15], (DEPTH, POOL_WIDTH)),
        "w_out": nrm(ks[16], (DEPTH, MIX_WIDTH, D_MODEL), MIX_WIDTH ** -0.5),
        "norm_ffn": gain(ks[17], (DEPTH, D_MODEL)),
        "w_gate": nrm(ks[18], (DEPTH, D_MODEL, D_FF), D_MODEL ** -0.5),
        "w_up": nrm(ks[19], (DEPTH, D_MODEL, D_FF), D_MODEL ** -0.5),
        "w_down": nrm(ks[20], (DEPTH, D_FF, D_MODEL), D_FF ** -0.5),
        "norm_final": gain(ks[21], (D_MODEL,)),
    }

def reference(x, norm_mix, w_in, lambda_re, lambda_im, log_step, b_re, b_im, c_re, c_im,
              d_skip, w_glu, b_glu, w_pool, b_pool, pool_scale, w_out, norm_ffn,
              w_gate, w_up, w_down, norm_final):
    out_dtype = x.dtype
    h_res = x.astype(jnp.float32)
    for l in range(DEPTH):
        h = rms_norm(h_res, norm_mix[l])
        proj = h @ w_in[l].astype(jnp.float32)
        u = proj[..., :SSM_WIDTH]
        v = proj[..., SSM_WIDTH:]
        y_ssm = s5_mixer(u, lambda_re[l], lambda_im[l], log_step[l], b_re[l], b_im[l],
                         c_re[l], c_im[l], d_skip[l], w_glu[l], b_glu[l])
        y_pool = pool_mixer(v, w_pool[l], b_pool[l], pool_scale[l])
        mixed = jnp.concatenate([y_ssm, y_pool], axis=-1)
        h_res = h_res + mixed @ w_out[l].astype(jnp.float32)
        h = rms_norm(h_res, norm_ffn[l])
        ff = jax.nn.silu(h @ w_gate[l].astype(jnp.float32)) * (h @ w_up[l].astype(jnp.float32))
        h_res = h_res + ff @ w_down[l].astype(jnp.float32)
    return rms_norm(h_res, norm_final).astype(out_dtype)


_drawn_inputs = setup_inputs


def setup_inputs(seed=0):
    import zlib

    import numpy as np

    out = dict(_drawn_inputs(seed))
    spreads = {}
    factors = {'norm_mix': 4.434,
     'lambda_re': 64.0,
     'lambda_im': 31.0,
     'log_step': 31.904,
     'b_re': 43.608,
     'b_im': 44.04,
     'c_re': 43.84,
     'c_im': 43.552,
     'b_glu': 186.409,
     'b_pool': 8.0,
     'pool_scale': 5.025,
     'norm_ffn': 12.511,
     'norm_final': 21.157}
    for name, (base, spread) in spreads.items():
        noise = np.random.default_rng([zlib.crc32(name.encode()), seed]).standard_normal(out[name].shape)
        drawn = base * np.exp(spread * noise) if base else spread * noise
        out[name] = __import__('jax').numpy.asarray(drawn.astype(out[name].dtype))
    for name, factor in factors.items():
        out[name] = (out[name] * factor).astype(out[name].dtype)
    return out
```

```python
import math
from contextlib import ExitStack

import concourse.bass as bass
from concourse import mybir

D_MODEL = 2048
SEQ = 512
SSM_WIDTH = 1024
GROUPS, STATE, GCH = 64, 64, 16
WINDOWS = (2, 4, 8, 16)
POOL_GROUP = 256
D_FF = ((8 * D_MODEL // 3 + 255) // 256) * 256
EPS = 1e-6

P = 128
KT = D_MODEL // P
NW = 512
CH = 8
NC = SEQ // CH
ROUNDS = 4
FG = D_FF // NW

RAW_SLOTS = 3
SPLIT_SLOTS = 3
PARAM_LOADS = 6 + 8 + 2 * (1 + 8) + 2


def emit(nc, x, norm_mix, w_in, lambda_re, lambda_im, log_step, b_re, b_im, c_re, c_im, d_skip,
         w_glu, b_glu, w_pool, b_pool, pool_scale, w_out, norm_ffn, w_gate, w_up, w_down,
         norm_final, out):
    f32, f32r, i32 = mybir.dt.float32, mybir.dt.float32r, mybir.dt.int32
    ALU, ACT, AX = mybir.AluOpType, mybir.ActivationFunctionType, mybir.AxisListType
    mult, add, sub = ALU.mult, ALU.add, ALU.subtract

    base = (nc.sbuf_base + 63) // 64 * 64
    end = nc.sbuf_usable_end

    def at(name, shape, dt, offset):
        size = 4
        for n in shape[1:]:
            size *= n
        assert offset + size <= end, (name, offset, size, end)
        return nc.alloc_sbuf_tensor_at(name, shape, dt, offset=offset)

    KB = 1024
    R_H = base
    R_A = R_H + 64 * KB
    R_W = R_A + 32 * KB
    R_S = R_W + RAW_SLOTS * 4 * KB + SPLIT_SLOTS * 8 * KB

    H_hi = at("H_hi", [P, KT, SEQ], f32r, R_H)
    H_lo = at("H_lo", [P, KT, SEQ], f32r, R_H + 32 * KB)
    x_tok = at("x_tok", [P, 4, D_MODEL], f32, R_A)
    UG = at("UG", [P, 8, CH, NC], f32, R_A)
    V = at("V", [P, 8, CH, NC], f32, R_A + 16 * KB)
    x_again = at("x_again", [P, 4, D_MODEL], f32, R_A)
    res_tok = at("res_tok", [P, 4, D_MODEL], f32, R_A)
    raw = [at(f"raw{i}", [P, 2, NW], f32, R_W + 4 * KB * i) for i in range(RAW_SLOTS)]
    R_W2 = R_W + RAW_SLOTS * 4 * KB
    w_hi = [at(f"w_hi{i}", [P, 2, NW], f32r, R_W2 + 8 * KB * i) for i in range(SPLIT_SLOTS)]
    w_lo = [at(f"w_lo{i}", [P, 2, NW], f32r, R_W2 + 8 * KB * i + 4 * KB) for i in range(SPLIT_SLOTS)]

    top = [R_S]

    def take(name, shape, dt=f32, part=P):
        size = 4
        for n in shape:
            size *= n
        t = at(name, [part, *shape], dt, top[0])
        top[0] += (size + 31) // 32 * 32
        return t

    ident = take("ident", [P])
    ones = take("ones", [P])
    vecs = take("vecs", [P])
    rstd = take("rstd", [SEQ])
    ssq = take("ssq", [4, 4])
    rtok = take("rtok", [4])
    vtok = take("vtok", [4])
    stok = take("stok", [4])
    inv_n = take("inv_n", [2, CH])
    R_T = top[0]
    mask = take("mask", [8, GCH])
    bb_re = take("bb_re", [4, 8, GCH])
    bb_im = take("bb_im", [4, 8, GCH])
    ct_re = take("ct_re", [4, 8, GCH])
    ct_in = take("ct_in", [4, 8, GCH])
    lp_re = take("lp_re", [CH + 1, 32])
    lp_im = take("lp_im", [CH + 1, 32])
    par = take("par", [24, 32])
    pari = take("pari", [32], i32)
    ph_c = take("ph_c", [32, NC])
    ph_s = take("ph_s", [32, NC])
    R_Q = top[0]
    QR = [take(f"q{k}", [8, CH, GCH]) for k in ("re", "im")]
    zr = take("zr", [8, NC])
    zi = take("zi", [8, NC])
    zt = take("zt", [8, NC])
    BD = take("BD", [2, CH, P])
    Q2 = [at(f"q2{k}", [P, CH, 8, GCH], f32, top[0] - 8 * KB + 4 * KB * n)
          for n, k in enumerate(("re", "im"))]
    R_QT = top[0]
    QT = take("QT", [2, 8, P])
    U8 = take("U8", [2, 8, NC])
    s_re = take("s_re", [8, NC + 1])
    s_im = take("s_im", [8, NC + 1])
    yt = at("yt", [64, CH, 2, P], f32, R_QT)
    tmp1024 = at("tmp1024", [P, 8, CH, GCH], f32, R_Q + 8 * KB)
    c_raw = [at(f"c_raw{k}", [P, 8, STATE], f32, R_Q + 2 * KB * k) for k in range(2)]
    b_raw = [at(f"b_raw{k}", [P, 4, 8, GCH], f32, R_QT + 2 * KB * k) for k in range(2)]
    t512 = [at(f"t512_{k}", [P, 32, GCH], f32, R_Q + 4 * KB + 2 * KB * k) for k in range(2)]
    pw = [at(f"pw{k}", [P, 4, 32], f32, R_Q + 4 * KB + 512 * k) for k in range(2)]
    pt = [at(f"pt{k}", [P, 32, 32], f32, R_Q + 4 * KB * k) for k in range(2)]
    vec_rows = at("vec_rows", [P, P], f32, R_QT + 4 * KB)
    lstep = at("lstep", [P, 4, 8], f32, R_QT + 5 * KB)
    sq_junk = at("sq_junk", [P, D_MODEL], f32, R_Q + 14 * KB)
    diag = at("diag", [P, 4, P], f32, R_Q + 8 * KB)


    M_hi = at("M_hi", [P, 8, SEQ], f32r, R_T)
    M_lo = at("M_lo", [P, 8, SEQ], f32r, R_T + 16 * KB)
    resT = at("resT", [P, KT, SEQ], f32, R_T + 32 * KB)
    gsig = at("gsig", [P, 4, SEQ], f32, R_T + 32 * KB)
    pmix = at("pmix", [P, 4, SEQ], f32, R_T + 40 * KB)
    sqt = at("sqt", [P, SEQ], f32, R_T + 64 * KB)
    sqa = at("sqa", [P, SEQ], f32, R_T + 66 * KB)
    assert top[0] <= R_T + 69 * KB
    top[0] = max(top[0], R_T + 68 * KB)
    pl = [take(f"pl{k}", [CH, NC]) for k in range(2)]
    pl_s = take("pl_s", [2, CH])
    F_hi = at("F_hi", [P, 4, SEQ], f32r, R_T)
    F_lo = at("F_lo", [P, 4, SEQ], f32r, R_T + 8 * KB)
    gate = at("gate", [P, 4, SEQ], f32, R_T + 16 * KB)
    fsq = at("fsq", [P, NW], f32, R_T + 24 * KB)
    gfin = at("gfin", [P, D_MODEL], f32, R_T + 32 * KB)
    u_dram = nc.dram_tensor("u_dram", (8, P, CH, NC), f32).ap()

    ctx = ExitStack()
    with ctx:
        ps = ctx.enter_context(nc.psum_tensor("ps", [P, 2, 4, 512], f32))

        def sem(name):
            return ctx.enter_context(nc.semaphore(name))

        free = [sem("half0_free"), sem("half1_free")]
        x_loaded = [sem(f"x_loaded{i}") for i in range(4)]
        raw_full = [sem(f"raw_full{i}") for i in range(RAW_SLOTS)]
        hi_done = sem("w_hi_done")
        lo_done = sem("w_lo_done")
        w_used = sem("w_used")
        aux_done = sem("aux_done")
        par_loaded = sem("par_loaded")
        u_stored = sem("u_stored")
        u8_loaded = sem("u8_loaded")
        xa_loaded = sem("x_again_loaded")
        gf_loaded = sem("gain_loaded")
        out_stored = sem("out_stored")
        consts = sem("consts_ready")
        x_hi = sem("x_hi")
        x_sq = sem("x_squares")
        trig_in = sem("trig_in")
        trig = sem("trig")
        chain = sem("dve_chain")
        gp_chain = sem("gp_chain")
        var_rdy = sem("mean_square_ready")
        root_done = sem("root_done")
        diag_rdy = sem("diag_ready")
        q_rdy = sem("q_ready")
        q2_rdy = sem("q2_ready")
        r_rdy = sem("r_ready")
        bd_rdy = sem("bd_ready")
        s_rdy = sem("s_ready")
        pooled = sem("pooled")
        pool_rdy = sem("pooled_split")
        g_rdy = sem("g_split")
        ms_rdy = sem("mixed_ssm_split")
        mp_rdy = sem("mixed_pool_split")
        h_rdy = sem("h_split")
        acc_rdy = sem("squares_ready")
        silu_done = sem("silu_done")
        scaled_rdy = sem("silu_scaled")
        ff_hi = sem("ff_hi")
        ff_rdy = sem("ff_split")
        fin_rdy = sem("final_tiles")
        fin_sq = sem("final_squares")
        o_rdy = sem("out_rows")

        jobs = {}
        uses = [0, 0]

        def job(name, half):
            jobs[name] = (half, uses[half], uses[half] + 1)
            uses[half] += 1

        job("vec", 0)
        for s in range(4):
            job(f"xt{s}", (s + 1) % 2)
        job("ct", 1)
        job("rms", 0)
        P_GLU, P_POOL, P_OUT, P_GATE, P_UP, P_LOOP = 32, 40, 42, 74, 82, 90
        PER = 24
        P_LAST = P_LOOP + PER * (FG - 1)
        assert PER % RAW_SLOTS == 0 and PER % SPLIT_SLOTS == 0
        small_after = {}
        for r in range(ROUNDS):
            p0 = 8 + 6 * r
            for kind, d in (("a", 0), ("b", 1), ("e", 1), ("i", 5), ("y", 6)):
                small_after.setdefault(min(p0 + d, P_GLU - 1), []).append((kind, r))
        for s in range(4):
            job(f"in{s}", (s + 1) % 2)
            for m in range(8):
                for kind, r in small_after.get(8 * s + m, []):
                    job(f"{kind}{r}", s % 2)
        for s in range(2):
            job(f"gl{s}", (s + 1) % 2)
        for s in range(2):
            job(f"po{s}", (s + 1) % 2)
        for s in range(4):
            job(f"wo{s}", (s + 1) % 2)
        job("gate", 1)
        job("rms2", 0)
        for t in range(4):
            job(f"tok{t}", (t + 1) % 2)
        job("up", 1)
        loop_uses = tuple(uses)
        LOOP = {"gate": (0, 0), "down0": (1, 0), "down1": (0, 1), "down2": (1, 1), "down3": (0, 2),
                "up": (1, 2)}
        aux_order = ["vec"] + [f"xt{s}" for s in range(4)] + ["ct", "rms"] \
            + [f"{kind}{r}" for pair in sorted(small_after) for kind, r in small_after[pair]] \
            + [f"wo{s}" for s in range(4)] + ["rms2"] + [f"tok{t}" for t in range(4)]
        aux_count = {name: n + 1 for n, name in enumerate(aux_order)}

        def wait_half(eng, name):
            half, need, _ = jobs[name]
            if need:
                eng.wait_ge(free[half], need)
            return half

        def wait_emptied(eng, name):
            half, _, then = jobs[name]
            eng.wait_ge(free[half], then)

        def wait_aux(eng, name):
            eng.wait_ge(aux_done, aux_count[name])

        def loop_free(name, i, after):
            half, nth = LOOP[name]
            return free[half], i * 3 + (loop_uses[half] + nth + after)

        def pair_src(w, rows, cols):
            return w[0, rows:rows + 2 * P, cols].rearrange("(k p) n -> p k n", p=P)

        def static_src(n):
            def cols(s):
                return slice(s * NW, (s + 1) * NW)
            if n < P_GLU:
                return pair_src(w_in, 256 * (n % 8), cols(n // 8))
            if n < P_POOL:
                s, m = divmod(n - P_GLU, 4)
                return pair_src(w_glu, 256 * m, cols(s))
            if n < P_OUT:
                m = n - P_POOL
                return w_pool[0, 2 * m:2 * m + 2, :, :].rearrange("g (k p) d -> p g k d", p=P)
            if n < P_GATE:
                s, m = divmod(n - P_OUT, 8)
                return pair_src(w_out, 256 * m, cols(s))
            if n < P_UP:
                return pair_src(w_gate, 256 * (n - P_GATE), cols(0))
            return pair_src(w_up, 256 * (n - P_UP), cols(0))

        block = ctx.enter_context(nc.Block())

        @block.sync
        def _(sp):
            def load(n, src, done=None):
                if n >= RAW_SLOTS:
                    sp.wait_ge(lo_done, n - RAW_SLOTS + 1 if done is None else done)
                dst = raw[n % RAW_SLOTS][:, :, :]
                if P_POOL <= n < P_OUT:
                    dst = dst.rearrange("p g (k d) -> p g k d", k=2)
                sp.dma_start(dst, src).then_inc(raw_full[n % RAW_SLOTS], 16)

            for t in range(4):
                for j in (2 * t, 2 * t + 1):
                    sp.dma_start(x_tok[64 * (j % 2):64 * (j % 2) + 64, t, :], x[0, j:SEQ:CH, :]) \
                        .then_inc(x_loaded[t], 16)
            for n in range(RAW_SLOTS):
                load(n, static_src(n))

            def store_u(r):
                wait_emptied(sp, f"in{r // 2}")
                sp.dma_start(u_dram[2 * r:2 * r + 2].rearrange("b p k c -> p b k c"),
                             UG[:, 2 * r:2 * r + 2, :, :]).then_inc(u_stored, 16)

            def load_u8(r):
                sp.wait_ge(u_stored, 32 * (r // 2 + 1))
                if r:
                    wait_aux(sp, f"e{r - 1}")
                for d in range(CH):
                    sp.dma_start(U8[16 * d:16 * d + 16, :, :, :],
                                 u_dram[2 * r:2 * r + 2, :, CH - 1 - d, :]
                                 .rearrange("q (g h) c -> h q g c", h=GCH)).then_inc(u8_loaded, 16)

            extra = {12: (0, 1), 20: (2, 3)}
            u8_at = {13: 0, 16: 1, 22: 2, 28: 3}
            for n in range(RAW_SLOTS, P_LOOP):
                load(n, static_src(n))
                for r in extra.get(n, ()):
                    store_u(r)
                if n in u8_at:
                    load_u8(u8_at[n])
                if n == P_OUT + 2:
                    sp.wait_ge(ms_rdy, 8)
                    sp.wait_ge(pool_rdy, 8)
                    for j in range(CH):
                        sp.dma_start(x_again[64 * (j % 2):64 * (j % 2) + 64, j // 2, :],
                                     x[0, j:SEQ:CH, :]).then_inc(xa_loaded, 16)

            with nc.sync.Fori(0, FG - 1) as i:
                for m in range(PER):
                    if m < 8:
                        src = w_gate[0, 256 * m:256 * m + 256, bass.ds(i * NW + NW, NW)]
                    elif m < 16:
                        c, kp = divmod(m - 8, 2)
                        src = w_down[0, bass.ds(i * NW + 256 * kp, 256), c * NW:(c + 1) * NW]
                    else:
                        src = w_up[0, 256 * (m - 16):256 * (m - 16) + 256, bass.ds(i * NW + NW, NW)]
                    load(P_LOOP + m, src.rearrange("(k p) n -> p k n", p=P),
                         done=i * PER + (P_LOOP + m - RAW_SLOTS + 1))
            for m in range(8):
                c, kp = divmod(m, 2)
                load(P_LAST + m, pair_src(w_down, (FG - 1) * NW + 256 * kp, slice(c * NW, (c + 1) * NW)))
            sp.dma_start(gfin[:, :], norm_final.partition_broadcast(P)).then_inc(gf_loaded, 16)
            for t in range(4):
                sp.wait_ge(o_rdy, t + 1)
                for j in (2 * t, 2 * t + 1):
                    sp.dma_start(out[0, j:SEQ:CH, :], res_tok[64 * (j % 2):64 * (j % 2) + 64, t, :]) \
                        .then_inc(out_stored, 16)
            sp.wait_ge(out_stored, 16 * CH)

        @block.scalar
        def _(act):
            def rows(v):
                return v.rearrange("o (r p) -> (o r) p", p=P)
            for src, r0, n in ((rows(norm_mix), 0, 16), (rows(norm_ffn), 16, 16), (rows(b_glu), 32, 8),
                               (b_pool.rearrange("o k (r p) -> (o k r) p", p=P), 40, 8),
                               (rows(pool_scale), 48, 8),
                               (d_skip.rearrange("o (r g) h -> (o r) (g h)", g=8), 56, 8)):
                act.dma_start(vec_rows[r0:r0 + n, :], src).then_inc(par_loaded, 16)
            for k, lam in enumerate((lambda_re, lambda_im)):
                for b in range(4):
                    r0 = 64 + 32 * k + 8 * b
                    act.dma_start(vec_rows[r0:r0 + 8, :].rearrange("g (q p) -> g q p", q=2),
                                  lam[0, 16 * b:16 * b + 16, :].rearrange("(q g) p -> g q p", q=2)) \
                        .then_inc(par_loaded, 16)
            for q in range(2):
                act.dma_start(lstep[64 * q:64 * q + 64, :, :],
                              log_step[0].rearrange("(b q g) -> q b g", q=2, g=8)[q]
                              .partition_broadcast(64)).then_inc(par_loaded, 16)
                for k, bm in enumerate((b_re, b_im)):
                    for b in range(4):
                        act.dma_start(b_raw[k][64 * q:64 * q + 64, b, :, :],
                                      bm[0, 16 * b + 8 * q:16 * b + 8 * q + 8, :, :]
                                      .rearrange("g p h -> p g h")).then_inc(par_loaded, 16)
            for k, cm in enumerate((c_re, c_im)):
                act.dma_start(c_raw[k][:, :, :],
                              cm[0].rearrange("(b g) h p -> (g h) b p", g=8)).then_inc(par_loaded, 16)

            def round_hi(n, full=None, used=None):
                act.wait_ge(raw_full[n % RAW_SLOTS], 16 * (n // RAW_SLOTS + 1) if full is None else full)
                if n >= SPLIT_SLOTS:
                    act.wait_ge(w_used, n - SPLIT_SLOTS + 1 if used is None else used)
                nc.scalar.copy(w_hi[n % SPLIT_SLOTS][:, :, :], raw[n % RAW_SLOTS][:, :, :]) \
                    .then_inc(hi_done, 1)

            wait_emptied(act, "vec")
            for s in range(4):
                wait_aux(act, f"xt{s}")
                half = jobs[f"xt{s}"][0]
                for b in range(4):
                    k = 4 * s + b
                    nc.scalar.activation(H_hi[:, k, :], ps[:, half, b, :], ACT.Copy,
                                         scale=vecs[:, k:k + 1]).then_inc(x_hi, 1)
                if s < SPLIT_SLOTS:
                    round_hi(s)
            for t in range(4):
                if t:
                    act.wait_ge(x_sq, t)
                nc.scalar.activation(sq_junk[:, :], x_tok[:, t, :], ACT.Square,
                                     accum_out=ssq[:, t, 0:1]).then_inc(x_sq, 1)
            act.wait_ge(var_rdy, 1)
            nc.scalar.activation(stok[:, :], vtok[:, :], ACT.Sqrt).then_inc(root_done, 1)
            act.wait_ge(trig_in, 1)
            nc.scalar.activation(par[:, 8, :], par[:, 6, :], ACT.Sin).then_inc(trig, 1)
            nc.scalar.activation(par[:, 9, :], par[:, 7, :], ACT.Sin).then_inc(trig, 1)

            def small(kind, r):
                half = jobs[f"{kind}{r}"][0]
                if kind == "a":
                    wait_aux(act, f"a{r}")
                    for b in range(4):
                        last = nc.scalar.copy(
                            QT[:, b // 2, 4 * (b % 2):4 * (b % 2) + 4, :],
                            ps[:, half, b, :].rearrange("p (g q) -> p g q", g=4))
                    last.then_inc(free[half], 1)
                elif kind == "i":
                    wait_aux(act, f"i{r}")
                    for b in range(4):
                        last = nc.scalar.copy(
                            yt[:, :, b // 2, 64 * (b % 2):64 * (b % 2) + 64]
                            .rearrange("c j (g h) -> c g j h", h=GCH),
                            ps[0:64, half, b, :].rearrange("c (g j h) -> c g j h", g=4, h=GCH))
                    last.then_inc(free[half], 1)
                elif kind == "y":
                    wait_aux(act, f"y{r}")
                    for q in range(2):
                        last = nc.scalar.activation(
                            UG[:, 2 * r + q, :, :], ps[:, half, q, :].rearrange("p (j c) -> p j c", j=CH),
                            ACT.Gelu)
                    last.then_inc(free[half], 1)

            for n in range(SPLIT_SLOTS, P_LOOP):
                round_hi(n)
                behind = n - SPLIT_SLOTS
                for kind, r in small_after.get(behind, []):
                    small(kind, r)
                for s in range(2):
                    if behind == P_GLU + 4 * s + 3:
                        act.wait_ge(w_used, behind + 1)
                        half = jobs[f"gl{s}"][0]
                        if s:
                            act.wait_ge(ms_rdy, 4)
                        for b in range(4):
                            last = nc.scalar.activation(gsig[:, b, :], ps[:, half, b, :], ACT.Sigmoid,
                                                        bias=vecs[:, 32 + 4 * s + b:33 + 4 * s + b])
                        last.then_inc(free[half], 1)
                if behind == P_GATE + 7:
                    act.wait_ge(var_rdy, 2)
                    nc.scalar.activation(sqt[:, :], sqa[:, :], ACT.Sqrt).then_inc(root_done, 1)
                    wait_emptied(act, "gate")
                    for b in range(4):
                        nc.scalar.activation(gate[:, b, :], gate[:, b, :], ACT.Silu).then_inc(silu_done, 1)
                    for t in range(4):
                        wait_aux(act, f"tok{t}")
                        half = jobs[f"tok{t}"][0]
                        for b in range(4):
                            last = nc.scalar.copy(res_tok[:, t, NW * b:NW * b + NW], ps[:, half, b, :])
                        last.then_inc(free[half], 1)

            with nc.scalar.Fori(0, FG - 1) as i:
                for m in range(PER):
                    n = P_LOOP + m
                    round_hi(n, full=i * (16 * PER // RAW_SLOTS) + 16 * (n // RAW_SLOTS + 1),
                             used=i * PER + (n - SPLIT_SLOTS + 1))
                    if m == 7 + SPLIT_SLOTS:
                        act.wait_ge(*loop_free("gate", i, 1))
                        for b in range(4):
                            nc.scalar.activation(gate[:, b, :], gate[:, b, :], ACT.Silu) \
                                .then_inc(silu_done, 1)
            for m in range(8):
                round_hi(P_LAST + m)
            for c in range(4):
                for t in range(4):
                    act.wait_ge(fin_rdy, 4 * c + t + 1)
                    if c or t:
                        act.wait_ge(fin_sq, 4 * c + t)
                    nc.scalar.activation(fsq[:, :], res_tok[:, t, NW * c:NW * c + NW], ACT.Square,
                                         accum_out=ssq[:, t, c:c + 1]).then_inc(fin_sq, 1)
            act.wait_ge(var_rdy, 3)
            nc.scalar.activation(stok[:, :], vtok[:, :], ACT.Sqrt).then_inc(root_done, 1)

        @block.gpsimd
        def _(gp):
            nc.gpsimd.memset(ident[:, :], 0.0).then_inc(consts, 1)
            nc.gpsimd.memset(ones[:, :], 1.0).then_inc(consts, 1)
            nc.gpsimd.memset(mask[:, :, :], 1.0).then_inc(consts, 1)
            gp.wait_ge(consts, 3)
            nc.gpsimd.affine_select(out=ident[:, :], in_=ident[:, :], compare_op=ALU.not_equal, fill=1.0,
                                    base=0, pattern=[[-1, P]], channel_multiplier=1).then_inc(consts, 1)
            nc.gpsimd.affine_select(out=mask[:, :, :], in_=mask[:, :, :], compare_op=ALU.is_ge, fill=0.0,
                                    base=0, pattern=[[-GCH, 8], [0, GCH]], channel_multiplier=1) \
                .then_inc(consts, 1)
            gp.wait_ge(consts, 5)
            nc.gpsimd.affine_select(out=mask[:, :, :], in_=mask[:, :, :], compare_op=ALU.is_ge, fill=0.0,
                                    base=GCH - 1, pattern=[[GCH, 8], [0, GCH]], channel_multiplier=-1) \
                .then_inc(consts, 1)
            for c in range(2):
                for j in range(CH):
                    nc.gpsimd.memset(inv_n[:, c, j:j + 1], 1.0 / (CH * c + j + 1)).then_inc(consts, 1)
            ALL_CONSTS = 6 + 2 * CH

            def rest_lo(n, done=None):
                gp.wait_ge(hi_done, n + 1 if done is None else done)
                nc.gpsimd.tensor_tensor(w_lo[n % SPLIT_SLOTS][:, :, :], raw[n % RAW_SLOTS][:, :, :],
                                        w_hi[n % SPLIT_SLOTS][:, :, :].bitcast(f32), sub) \
                    .then_inc(lo_done, 1)

            steps = [0]

            def step(ins):
                steps[0] += 1
                ins.then_inc(gp_chain, 1)

            def settle():
                gp.wait_ge(gp_chain, steps[0])

            def shifted_add(o, a, s):
                if s < CH:
                    step(nc.gpsimd.tensor_tensor(o[:, s:, :], a[:, s:, :], a[:, :CH - s, :], add))
                    step(nc.gpsimd.tensor_tensor(o[:, 0:s, 1:], a[:, 0:s, 1:], a[:, CH - s:, :NC - 1], add))
                    step(nc.gpsimd.tensor_copy(o[:, 0:s, 0:1], a[:, 0:s, 0:1]))
                else:
                    step(nc.gpsimd.tensor_tensor(o[:, :, 1:], a[:, :, 1:], a[:, :, :NC - 1], add))
                    step(nc.gpsimd.tensor_copy(o[:, :, 0:1], a[:, :, 0:1]))
                settle()

            def finish(k, w, cur):
                v = V[:, k, :, :]
                nj, ncol = min(w, CH), max(1, w // CH)
                for c in range(ncol):
                    step(nc.gpsimd.tensor_tensor(pl_s[:, c, 0:nj], cur[:, 0:nj, c], inv_n[:, c, 0:nj], mult))
                settle()
                step(nc.gpsimd.tensor_scalar(cur, cur, 1.0 / w, None, mult))
                for c in range(ncol):
                    step(nc.gpsimd.tensor_tensor(pl_s[:, c, 0:nj], pl_s[:, c, 0:nj], v[:, 0:nj, c], sub))
                settle()
                step(nc.gpsimd.tensor_tensor(v, cur, v, sub))
                settle()
                for c in range(ncol):
                    ins = nc.gpsimd.tensor_copy(v[:, 0:nj, c], pl_s[:, c, 0:nj])
                    if c < ncol - 1:
                        step(ins)
                ins.then_inc(pooled, 1)
                gp.wait_ge(pooled, k + 1)

            pieces = [(k, s) for k in range(8) for s in (1, 2, 4, 8, 0) if s < WINDOWS[k // 2]]

            def piece(k, s):
                src = V[:, k, :, :]
                if s > 1 or s == 0:
                    level = (s if s else WINDOWS[k // 2]).bit_length() - 2
                    src = pl[level % 2][:, :, :]
                if s:
                    shifted_add(pl[(s.bit_length() - 1) % 2], src, s)
                else:
                    finish(k, WINDOWS[k // 2], src)

            V0_PIECES = sum(1 for k, _ in pieces if k < 4)
            gp.wait_ge(consts, ALL_CONSTS)
            at_piece = 0
            for n in range(P_LOOP):
                rest_lo(n)
                if n >= 28 and at_piece < len(pieces):
                    todo = 2 if n < 34 else 1
                    for _ in range(todo):
                        if at_piece >= len(pieces):
                            break
                        if at_piece == 0:
                            wait_emptied(gp, "in2")
                        if at_piece == V0_PIECES:
                            if n < 34:
                                break
                            wait_emptied(gp, "in3")
                        piece(*pieces[at_piece])
                        at_piece += 1
                if n == 36:
                    while at_piece < len(pieces):
                        piece(*pieces[at_piece])
                        at_piece += 1
            with nc.gpsimd.Fori(0, FG - 1) as i:
                for m in range(PER):
                    rest_lo(P_LOOP + m, i * PER + (P_LOOP + m + 1))
            for m in range(8):
                rest_lo(P_LAST + m)

        @block.vector
        def _(dve):
            steps = [0]

            def step(ins):
                steps[0] += 1
                ins.then_inc(chain, 1)

            def settle():
                dve.wait_ge(chain, steps[0])

            def tt(o, a, b, op):
                step(nc.vector.tensor_tensor(o, a, b, op))

            def ts(o, a, s1, s2, op0, op1=None):
                if op1 is None:
                    step(nc.vector.tensor_scalar(o, a, s1, None, op0))
                else:
                    step(nc.vector.tensor_scalar(o, a, s1, s2, op0, op1))

            def stt(o, a, s, b, op0, op1):
                step(nc.vector.scalar_tensor_tensor(out=o, in0=a, scalar=s, in1=b, op0=op0, op1=op1))

            def inverse_root(y, var, root, nth):
                dve.wait_ge(root_done, nth)
                step(nc.vector.reciprocal(y, root))
                settle()
                tt(root, y, y, mult)
                settle()
                tt(root, root, var, mult)
                settle()
                ts(root, root, -0.5, 1.5, mult, add)
                settle()
                tt(y, y, root, mult)
                settle()

            wait_aux(dve, "vec")
            nc.vector.tensor_copy(vecs[:, :], ps[:, 0, 0, 0:P]).then_inc(free[0], 1)
            wait_emptied(dve, "vec")
            for s in range(4):
                wait_aux(dve, f"xt{s}")
                half = jobs[f"xt{s}"][0]
                for b in range(4):
                    k = 4 * s + b
                    dve.wait_ge(x_hi, k + 1)
                    last = nc.vector.scalar_tensor_tensor(
                        out=H_lo[:, k, :], in0=ps[:, half, b, :], scalar=vecs[:, k:k + 1],
                        in1=H_hi[:, k, :].bitcast(f32), op0=mult, op1=sub)
                last.then_inc(free[half], 1)
            wait_aux(dve, "ct")
            half = jobs["ct"][0]
            step(nc.vector.tensor_copy(ct_re[:, :, :, :].rearrange("p b g h -> p (b g h)"),
                                       ps[:, half, 0, :]))
            nc.vector.tensor_scalar(ct_in[:, :, :, :].rearrange("p b g h -> p (b g h)"),
                                    ps[:, half, 1, :], -1.0, None, mult).then_inc(free[half], 1)
            wait_emptied(dve, "ct")
            dve.wait_ge(x_sq, 4)
            nc.vector.tensor_scalar(vtok[:, :], ssq[:, :, 0], 1.0 / D_MODEL, EPS, mult, add) \
                .then_inc(var_rdy, 1)
            inverse_root(rtok[:, :], vtok[:, :], stok[:, :], 1)
            dve.wait_ge(consts, 6)
            for t in range(4):
                nc.vector.tensor_scalar(diag[:, t, :], ident[:, :], rtok[:, t:t + 1], None, mult) \
                    .then_inc(diag_rdy, 1)
            wait_aux(dve, "rms")
            half = jobs["rms"][0]
            nc.vector.tensor_copy(rstd[:, :], ps[:, half, 0, :]).then_inc(free[half], 1)
            wait_emptied(dve, "rms")

            lr, li = vecs[:, 64:96], vecs[:, 96:128]
            v_ = [par[:, k, :] for k in range(24)]
            LOG2E, MAGIC = 1.0 / math.log(2.0), 1.5 * 2.0 ** 23
            LN2_HI = 0.693145751953125
            LN2_LO = math.log(2.0) - LN2_HI

            def exp_parts(src, two_n, f, em1):
                ts(f, src, -88.0, 88.0, ALU.max, ALU.min)
                settle()
                ts(two_n, f, LOG2E, MAGIC, mult, add)
                settle()
                ts(two_n, two_n, MAGIC, None, sub)
                settle()
                stt(f, two_n, -LN2_HI, f, mult, add)
                settle()
                stt(f, two_n, -LN2_LO, f, mult, add)
                settle()
                ts(em1, f, 1.0 / 5040, None, mult)
                for c in (720, 120, 24, 6, 2, 1):
                    settle()
                    stt(em1, em1, 1.0 / c, f, add, mult)
                ts(pari[:, :], two_n, 127.0, 2.0 ** 23, add, mult)
                settle()
                step(nc.vector.tensor_copy(two_n, pari[:, :].bitcast(f32)))
                settle()

            exp_parts(lstep[:, :, :].rearrange("p b g -> p (b g)"), v_[0], v_[1], v_[2])
            tt(v_[3], v_[2], v_[0], mult)
            settle()
            tt(v_[3], v_[3], v_[0], add)
            settle()
            tt(v_[4], lr, v_[3], mult)
            tt(v_[5], li, v_[3], mult)
            settle()
            ts(v_[0], v_[5], 1.0 / (2 * math.pi), MAGIC, mult, add)
            settle()
            ts(v_[0], v_[0], MAGIC, None, sub)
            settle()
            c1, c2 = 6.28125, 0.00193500518798828125
            for c in (c1, c2, 2 * math.pi - c1 - c2):
                stt(v_[5], v_[0], -c, v_[5], mult, add)
                settle()
            ts(v_[6], v_[5], 0.5, None, mult)
            settle()
            ts(v_[6], v_[6], -math.pi / 2, math.pi / 2, ALU.max, ALU.min)
            settle()
            ts(v_[7], v_[6], -1.0, None, mult)
            settle()
            tt(v_[7], v_[7], v_[6], ALU.min)
            settle()
            nc.vector.tensor_scalar(v_[7], v_[7], math.pi / 2, None, add).then_inc(trig_in, 1)
            exp_parts(v_[4], v_[0], v_[1], v_[2])
            tt(v_[11], v_[2], v_[0], mult)
            settle()
            tt(v_[10], v_[11], v_[0], add)
            stt(v_[11], v_[0], -1.0, v_[11], add, add)
            dve.wait_ge(trig, 2)
            tt(v_[12], v_[8], v_[9], mult)
            tt(v_[13], v_[8], v_[8], mult)
            settle()
            ts(v_[12], v_[12], 2.0, None, mult)
            ts(v_[14], v_[13], -2.0, 1.0, mult, add)
            settle()
            ts(v_[13], v_[13], -2.0, None, mult)
            step(nc.vector.memset(lp_re[:, 0, :], 1.0))
            step(nc.vector.memset(lp_im[:, 0, :], 0.0))
            tt(lp_re[:, 1, :], v_[10], v_[14], mult)
            tt(lp_im[:, 1, :], v_[10], v_[12], mult)
            tt(v_[15], v_[11], v_[14], mult)
            tt(v_[16], lr, lr, mult)
            tt(v_[17], li, li, mult)
            settle()
            tt(v_[15], v_[15], v_[13], add)
            tt(v_[16], v_[16], v_[17], add)
            settle()
            step(nc.vector.reciprocal(v_[21], v_[16]))
            tt(v_[17], v_[15], lr, mult)
            tt(v_[18], lp_im[:, 1, :], li, mult)
            tt(v_[19], lp_im[:, 1, :], lr, mult)
            tt(v_[20], v_[15], li, mult)
            settle()
            tt(v_[17], v_[17], v_[18], add)
            tt(v_[19], v_[19], v_[20], sub)
            settle()
            tt(v_[17], v_[17], v_[21], mult)
            tt(v_[19], v_[19], v_[21], mult)
            settle()

            def cmul(o, a, b, t1, t2):
                tt(o[0], a[0], b[0], mult)
                tt(t1, a[1], b[1], mult)
                tt(o[1], a[0], b[1], mult)
                tt(t2, a[1], b[0], mult)
                settle()
                tt(o[0], o[0], t1, sub)
                tt(o[1], o[1], t2, add)
                settle()

            def cols(v, n):
                return v.unsqueeze(2).to_broadcast([P, 32, n])

            def by_state(t):
                return t[:, :, :, :].rearrange("p b g h -> p (b g) h")

            cmul((by_state(bb_re), by_state(bb_im)), (cols(v_[17], GCH), cols(v_[19], GCH)),
                 (by_state(b_raw[0]), by_state(b_raw[1])), t512[0][:, :, :], t512[1][:, :, :])
            for first, n, by in ((2, 1, 1), (3, 2, 2), (5, 4, 4)):
                fac = [t[:, by, :].unsqueeze(1).to_broadcast([P, n, 32]) for t in (lp_re, lp_im)]
                cmul((lp_re[:, first:first + n, :], lp_im[:, first:first + n, :]),
                     (lp_re[:, 1:1 + n, :], lp_im[:, 1:1 + n, :]), fac,
                     pw[0][:, 0:n, :], pw[1][:, 0:n, :])

            def square_phase():
                tt(v_[0], v_[14], v_[14], mult)
                tt(v_[1], v_[12], v_[12], mult)
                tt(v_[2], v_[14], v_[12], mult)
                settle()
                tt(v_[14], v_[0], v_[1], sub)
                ts(v_[12], v_[2], 2.0, None, mult)
                settle()

            for _ in range(3):
                tt(v_[10], v_[10], v_[10], mult)
                square_phase()
            step(nc.vector.memset(ph_c[:, :, 0:1], 1.0))
            step(nc.vector.memset(ph_s[:, :, 0:1], 0.0))
            settle()
            n = 1
            while n < NC:
                cmul((ph_c[:, :, n:2 * n], ph_s[:, :, n:2 * n]), (ph_c[:, :, 0:n], ph_s[:, :, 0:n]),
                     (cols(v_[14], n), cols(v_[12], n)), pt[0][:, :, 0:n], pt[1][:, :, 0:n])
                n *= 2
                if n < NC:
                    square_phase()
            step(nc.vector.memset(s_re[:, :, 0:1], 0.0))
            step(nc.vector.memset(s_im[:, :, 0:1], 0.0))
            settle()

            shape4 = [P, 8, CH, GCH]
            tmp = tmp1024[:, :, :, :]
            Q_re, Q_im = QR[0][:, :, :, :], QR[1][:, :, :, :]

            def power(t, first, r):
                return t[:, first:first + CH, 8 * r:8 * r + 8].rearrange("p d g -> p g d") \
                    .unsqueeze(3).to_broadcast(shape4)

            def chan(t, r):
                return t[:, r, :, :].unsqueeze(2).to_broadcast(shape4)

            def build_q(r):
                if r:
                    wait_aux(dve, f"i{r - 1}")
                tt(Q_re, power(lp_re, 0, r), chan(bb_re, r), mult)
                tt(tmp, power(lp_im, 0, r), chan(bb_im, r), mult)
                settle()
                tt(Q_re, Q_re, tmp, sub)
                tt(Q_im, power(lp_re, 0, r), chan(bb_im, r), mult)
                settle()
                tt(tmp, power(lp_im, 0, r), chan(bb_re, r), mult)
                settle()
                nc.vector.tensor_tensor(Q_im, Q_im, tmp, add).then_inc(q_rdy, 1)
                dve.wait_ge(q_rdy, r + 1)
                if r:
                    wait_aux(dve, f"y{r - 1}")
                for k in range(2):
                    nc.vector.tensor_copy(Q2[k][:, :, :, :].rearrange("p d g h -> p g d h"),
                                          QR[k][:, :, :, :]).then_inc(q2_rdy, 1)

            def build_r(r):
                wait_aux(dve, f"b{r}")
                tt(Q_re, power(lp_re, 1, r), chan(ct_re, r), mult)
                tt(tmp, power(lp_im, 1, r), chan(ct_in, r), mult)
                settle()
                tt(Q_re, Q_re, tmp, add)
                tt(Q_im, power(lp_re, 1, r), chan(ct_in, r), mult)
                settle()
                tt(tmp, power(lp_im, 1, r), chan(ct_re, r), mult)
                settle()
                nc.vector.tensor_tensor(Q_im, Q_im, tmp, sub).then_inc(r_rdy, 1)
                dve.wait_ge(r_rdy, r + 1)

            def taps(r):
                wait_aux(dve, f"b{r}")
                half = jobs[f"b{r}"][0]
                mk = mask[:, :, :].rearrange("p g h -> p (g h)").unsqueeze(1).to_broadcast([P, 4, P])
                for b in range(4):
                    ins = nc.vector.tensor_tensor(
                        BD[:, b // 2, 4 * (b % 2):4 * (b % 2) + 4, :],
                        ps[:, half, b, :].rearrange("p (d m) -> p d m", d=4), mk, mult)
                    if b < 3:
                        step(ins)
                ins.then_inc(free[half], 1)
                settle()
                for q in range(2):
                    k = 56 + 2 * r + q
                    nc.vector.scalar_tensor_tensor(out=BD[:, q, 0, :], in0=ident[:, :],
                                                   scalar=vecs[:, k:k + 1], in1=BD[:, q, 0, :],
                                                   op0=mult, op1=add).then_inc(bd_rdy, 1)

            def states(r):
                wait_aux(dve, f"e{r}")
                half = jobs[f"e{r}"][0]
                pc, pn = ph_c[:, 8 * r:8 * r + 8, :], ph_s[:, 8 * r:8 * r + 8, :]
                e_re = ps[:, half, 0, :].rearrange("p (g c) -> p g c", g=8)
                e_im = ps[:, half, 1, :].rearrange("p (g c) -> p g c", g=8)
                ZR, ZI, ZT = zr[:, :, :], zi[:, :, :], zt[:, :, :]
                tt(ZR, e_re, pc, mult)
                tt(ZT, e_im, pn, mult)
                settle()
                tt(ZR, ZR, ZT, add)
                tt(ZI, e_im, pc, mult)
                settle()
                nc.vector.tensor_tensor(ZT, e_re, pn, mult).then_inc(free[half], 1)
                wait_emptied(dve, f"e{r}")
                tt(ZI, ZI, ZT, sub)
                settle()
                for z in (zr, zi):
                    for g in range(8):
                        rho = v_[10][:, 8 * r + g:8 * r + g + 1].to_broadcast([P, NC])
                        step(nc.vector.tensor_tensor_scan(z[:, g, :], rho, z[:, g, :], 0.0, mult, add))
                settle()
                S_re, S_im = s_re[:, :, 1:], s_im[:, :, 1:]
                tt(S_re, ZR, pc, mult)
                tt(ZT, ZI, pn, mult)
                settle()
                tt(S_re, S_re, ZT, sub)
                tt(S_im, ZI, pc, mult)
                settle()
                tt(ZT, ZR, pn, mult)
                settle()
                nc.vector.tensor_tensor(S_im, S_im, ZT, add).then_inc(s_rdy, 1)
                dve.wait_ge(s_rdy, r + 1)

            def small(kind, r):
                if kind == "b":
                    taps(r)
                    build_r(r)
                elif kind == "e":
                    states(r)
                elif kind == "i" and r + 1 < ROUNDS:
                    build_q(r + 1)

            def split_tile(src, hi, lo, done):
                step(nc.vector.tensor_copy(hi, src))
                settle()
                nc.vector.tensor_tensor(lo, src, hi.bitcast(f32), sub).then_inc(done, 1)

            build_q(0)
            for pair in range(P_GLU):
                if pair % 8 == 7:
                    s = pair // 8
                    dve.wait_ge(w_used, pair + 1)
                    half = jobs[f"in{s}"][0]
                    dst = (UG, V)[s // 2][:, 4 * (s % 2):4 * (s % 2) + 4, :, :]
                    for b in range(4):
                        ins = nc.vector.tensor_tensor(
                            dst[:, b, :, :], ps[:, half, b, :].rearrange("p (j c) -> p j c", j=CH),
                            rstd[:, :].rearrange("p (j c) -> p j c", j=CH), mult)
                    ins.then_inc(free[half], 1)
                for kind, r in small_after.get(pair, []):
                    small(kind, r)

            for k in range(8):
                wait_emptied(dve, f"y{k // 2}")
                split_tile(UG[:, k, :, :].rearrange("p j c -> p (j c)"), H_hi[:, k, :], H_lo[:, k, :],
                           g_rdy)
            for k in range(4):
                dve.wait_ge(pooled, k + 1)
                split_tile(V[:, k, :, :].rearrange("p j c -> p (j c)"), H_hi[:, 8 + k, :],
                           H_lo[:, 8 + k, :], pool_rdy)
            for s in range(2):
                wait_emptied(dve, f"gl{s}")
                for b in range(4):
                    k = 4 * s + b
                    tt(gsig[:, b, :], gsig[:, b, :], UG[:, k, :, :].rearrange("p j c -> p (j c)"), mult)
                settle()
                for b in range(4):
                    k = 4 * s + b
                    split_tile(gsig[:, b, :], M_hi[:, k, :], M_lo[:, k, :], ms_rdy)
                if s == 0:
                    for k in range(4, 8):
                        dve.wait_ge(pooled, k + 1)
                        split_tile(V[:, k, :, :].rearrange("p j c -> p (j c)"), H_hi[:, 8 + k, :],
                                   H_lo[:, 8 + k, :], pool_rdy)
            for s in range(2):
                dve.wait_ge(w_used, P_POOL + s + 1)
                if s:
                    dve.wait_ge(mp_rdy, 4)
                half = jobs[f"po{s}"][0]
                for b in range(4):
                    k = 4 * s + b
                    ins = nc.vector.tensor_scalar(pmix[:, b, :], ps[:, half, b, :], vecs[:, 40 + k:41 + k],
                                                  vecs[:, 48 + k:49 + k], add, mult)
                ins.then_inc(free[half], 1)
                wait_emptied(dve, f"po{s}")
                for b in range(4):
                    split_tile(pmix[:, b, :], H_hi[:, 4 * s + b, :], H_lo[:, 4 * s + b, :], mp_rdy)
            dve.wait_ge(mp_rdy, 8)

            def ffn_input(k):
                g = vecs[:, 16 + k:17 + k]
                ts(H_hi[:, (k + 8) % 16, :], resT[:, k, :], g, None, mult)
                settle()
                nc.vector.scalar_tensor_tensor(out=H_lo[:, (k + 8) % 16, :], in0=resT[:, k, :], scalar=g,
                                               in1=H_hi[:, (k + 8) % 16, :].bitcast(f32),
                                               op0=mult, op1=sub).then_inc(h_rdy, 1)

            def add_square(k):
                tt(sqa[:, :] if k == 0 else sqt[:, :], resT[:, k, :], resT[:, k, :], mult)
                settle()
                if k:
                    ins = nc.vector.tensor_tensor(sqa[:, :], sqa[:, :], sqt[:, :], add)
                    if k < KT - 1:
                        step(ins)
                        settle()
                    else:
                        ins.then_inc(acc_rdy, 1)

            for s in range(4):
                wait_aux(dve, f"wo{s}")
                half = jobs[f"wo{s}"][0]
                for b in range(4):
                    ins = nc.vector.tensor_copy(resT[:, 4 * s + b, :], ps[:, half, b, :])
                ins.then_inc(free[half], 1)
                wait_emptied(dve, f"wo{s}")
                if s < 2:
                    for b in range(4):
                        ffn_input(4 * s + b)
                if s == 3:
                    for k in range(8, 16):
                        ffn_input(k)
                for b in range(4):
                    add_square(4 * s + b)
            wait_aux(dve, "rms2")
            half = jobs["rms2"][0]
            nc.vector.tensor_copy(sqt[:, :], ps[:, half, 0, :]).then_inc(free[half], 1)
            wait_emptied(dve, "rms2")
            nc.vector.tensor_scalar(sqa[:, :], sqt[:, :], 1.0 / D_MODEL, EPS, mult, add) \
                .then_inc(var_rdy, 1)
            inverse_root(rstd[:, :], sqa[:, :], sqt[:, :], 2)

            def gate_out(half, used, freed_wait, silu):
                dve.wait_ge(w_used, used)
                for b in range(4):
                    ins = nc.vector.tensor_tensor(gate[:, b, :], ps[:, half, b, :], rstd[:, :], mult)
                ins.then_inc(free[half], 1)

            def gate_scale(first):
                for b in range(4):
                    dve.wait_ge(silu_done, first + b)
                    nc.vector.tensor_tensor(gate[:, b, :], gate[:, b, :], rstd[:, :], mult) \
                        .then_inc(scaled_rdy, 1)

            def up_out(half, used, freed, scaled, ff):
                dve.wait_ge(w_used, used)
                dve.wait_ge(scaled_rdy, scaled)
                for b in range(4):
                    ins = nc.vector.tensor_tensor(gate[:, b, :], ps[:, half, b, :], gate[:, b, :], mult)
                ins.then_inc(free[half], 1)
                dve.wait_ge(*freed)
                for b in range(4):
                    nc.vector.tensor_copy(F_hi[:, b, :], gate[:, b, :]).then_inc(ff_hi, 1)
                for b in range(4):
                    dve.wait_ge(ff_hi, ff + b)
                    nc.vector.tensor_tensor(F_lo[:, b, :], gate[:, b, :], F_hi[:, b, :].bitcast(f32), sub) \
                        .then_inc(ff_rdy, 1)

            gate_out(jobs["gate"][0], P_UP, None, None)
            gate_scale(1)
            half, _, then = jobs["up"]
            up_out(half, P_LOOP, (free[half], then), 4, 1)
            wait_emptied(dve, "tok3")
            with nc.vector.Fori(0, FG - 1) as i:
                dve.wait_ge(ff_rdy, i * 4 + 4)
                gate_out(0, i * PER + (P_LOOP + 8), None, None)
                for c in range(4):
                    half = LOOP[f"down{c}"][0]
                    dve.wait_ge(w_used, i * PER + (P_LOOP + 8 + 2 * c + 2))
                    for t in range(4):
                        cell = res_tok[:, t, NW * c:NW * c + NW]
                        ins = nc.vector.tensor_tensor(cell, ps[:, half, t, :], cell, add)
                    ins.then_inc(free[half], 1)
                    if c == 2:
                        gate_scale(i * 4 + 5)
                up_out(1, i * PER + (P_LOOP + PER), loop_free("up", i, 1), i * 4 + 8, i * 4 + 5)
            for c in range(4):
                half = c % 2
                dve.wait_ge(w_used, P_LAST + 2 * c + 2)
                for t in range(4):
                    cell = res_tok[:, t, NW * c:NW * c + NW]
                    nc.vector.tensor_tensor(cell, ps[:, half, t, :], cell, add).then_inc(fin_rdy, 1)
            dve.wait_ge(fin_sq, 16)
            step(nc.vector.tensor_reduce(rtok[:, :], ssq[:, :, :], AX.X, add))
            settle()
            nc.vector.tensor_scalar(vtok[:, :], rtok[:, :], 1.0 / D_MODEL, EPS, mult, add) \
                .then_inc(var_rdy, 1)
            inverse_root(rtok[:, :], vtok[:, :], stok[:, :], 3)
            dve.wait_ge(gf_loaded, 16)
            for t in range(4):
                nc.vector.scalar_tensor_tensor(out=res_tok[:, t, :], in0=res_tok[:, t, :],
                                               scalar=rtok[:, t:t + 1], in1=gfin[:, :],
                                               op0=mult, op1=mult).then_inc(o_rdy, 1)

        @block.tensor
        def _(pe):
            mm = nc.tensor.matmul

            def three(o, w, w_cols, act_, k, first, last, stationary_is_w=True):
                (wh, wl), (ah, al) = w, act_
                ins = None
                for n_, (a, b) in enumerate(((wh, ah), (wh, al), (wl, ah)) if stationary_is_w
                                            else ((ah, wh), (ah, wl), (al, wh))):
                    ins = mm(o, a, b, start=first and n_ == 0, stop=last and n_ == 2)
                return ins

            def weight_pair(n, half, acts, first, last, split=None, used_inc=True):
                wh, wl = w_hi[n % SPLIT_SLOTS], w_lo[n % SPLIT_SLOTS]
                for kt in range(2):
                    for b in range(4):
                        cs = slice(P * b, P * b + P)
                        ins = three(ps[:, half, b, :], (wh[:, kt, cs], wl[:, kt, cs]), None, acts[kt], None,
                                    first and kt == 0, last and kt == 1)
                return ins

            def h_at(k):
                return H_hi[:, k, :], H_lo[:, k, :]

            def m_at(k):
                return M_hi[:, k, :], M_lo[:, k, :]

            pe.wait_ge(consts, 6)
            pe.wait_ge(par_loaded, 16 * PARAM_LOADS)
            half = wait_half(pe, "vec")
            nc.tensor.transpose(ps[:, half, 0, 0:P], vec_rows[:, :], ident[:, :]).then_inc(aux_done, 1)
            for t in range(4):
                pe.wait_ge(x_loaded[t], 32)
            for s in range(4):
                half = wait_half(pe, f"xt{s}")
                for b in range(4):
                    for t in range(4):
                        k = 4 * s + b
                        ins = nc.tensor.transpose(ps[:, half, b, P * t:P * t + P],
                                                  x_tok[:, t, P * k:P * k + P], ident[:, :])
                ins.then_inc(aux_done, 1)
            half = wait_half(pe, "ct")
            for k in range(2):
                for b in range(4):
                    ins = nc.tensor.transpose(ps[:, half, k, P * b:P * b + P],
                                              c_raw[k][:, 2 * b:2 * b + 2, :].rearrange("p b s -> p (b s)"),
                                              ident[:, :])
            ins.then_inc(aux_done, 1)
            half = wait_half(pe, "rms")
            pe.wait_ge(diag_rdy, 4)
            mm(ps[:, half, 0, :], ones[:, :], diag[:, :, :].rearrange("p t n -> p (t n)"),
               start=True, stop=True).then_inc(aux_done, 1)

            def small(kind, r):
                half = wait_half(pe, f"{kind}{r}")
                if kind == "a":
                    pe.wait_ge(q_rdy, r + 1)
                    for k in range(2):
                        for g in range(8):
                            ins = nc.tensor.transpose(
                                ps[:, half, 2 * k + g // 4, P * (g % 4):P * (g % 4) + P],
                                QR[k][:, g, :, :].rearrange("p d h -> p (d h)"), ident[:, :])
                elif kind == "b":
                    pe.wait_ge(q2_rdy, 2 * (r + 1))
                    for q in range(2):
                        rows = slice(64 * q, 64 * q + 64)
                        for d in range(CH):
                            o = ps[:, half, 2 * q + d // 4, P * (d % 4):P * (d % 4) + P]
                            mm(o, Q2[0][rows, d, :, :].rearrange("p g h -> p (g h)"), ct_re[rows, r, :, :].rearrange("p g h -> p (g h)"),
                               start=True, stop=False)
                            ins = mm(o, Q2[1][rows, d, :, :].rearrange("p g h -> p (g h)"),
                                     ct_in[rows, r, :, :].rearrange("p g h -> p (g h)"),
                                     start=False, stop=True)
                elif kind == "e":
                    wait_emptied(pe, f"a{r}")
                    pe.wait_ge(u8_loaded, 16 * CH * (r + 1))
                    for k in range(2):
                        for q in range(2):
                            rows = slice(64 * q, 64 * q + 64)
                            for g in range(8):
                                ins = mm(ps[rows, half, k, NC * g:NC * g + NC], QT[:, k, g, rows],
                                         U8[:, q, g, :], start=True, stop=True)
                elif kind == "i":
                    pe.wait_ge(s_rdy, r + 1)
                    pe.wait_ge(r_rdy, r + 1)
                    for q in range(2):
                        rows = slice(64 * q, 64 * q + 64)
                        for g in range(8):
                            o = ps[0:64, half, 2 * q + g // 4, P * (g % 4):P * (g % 4) + P]
                            for k, st in enumerate((s_re, s_im)):
                                ins = mm(o, st[rows, g, 0:NC],
                                         QR[k][rows, g, :, :].rearrange("p j h -> p (j h)"),
                                         start=k == 0, stop=k == 1)
                elif kind == "y":
                    wait_emptied(pe, f"i{r}")
                    pe.wait_ge(bd_rdy, 2 * (r + 1))
                    for q in range(2):
                        o = ps[:, half, q, :]
                        for d in range(CH):
                            mm(o[:, NC * d:], BD[:, q, d, :],
                               UG[:, 2 * r + q, 0:CH - d, :].rearrange("p j c -> p (j c)"),
                               start=d == 0, stop=False)
                        for j in range(CH):
                            ins = mm(o[:, NC * j:NC * j + NC], yt[:, j, q, :], ident[0:64, 0:NC],
                                     start=False, stop=j == CH - 1)
                ins.then_inc(aux_done, 1)

            for n in range(P_GLU):
                s, m = divmod(n, 8)
                half = jobs[f"in{s}"][0]
                if m == 0:
                    wait_half(pe, f"in{s}")
                if s == 0 and m % 2 == 0:
                    wait_emptied(pe, f"xt{m // 2}")
                pe.wait_ge(lo_done, n + 1)
                weight_pair(n, half, (h_at(2 * m), h_at(2 * m + 1)), m == 0, m == 7).then_inc(w_used, 1)
                for kind, r in small_after.get(n, []):
                    small(kind, r)
            for n in range(P_GLU, P_POOL):
                s, m = divmod(n - P_GLU, 4)
                half = jobs[f"gl{s}"][0]
                if m == 0:
                    wait_half(pe, f"gl{s}")
                if s == 0:
                    pe.wait_ge(g_rdy, 2 * m + 2)
                pe.wait_ge(lo_done, n + 1)
                weight_pair(n, half, (h_at(2 * m), h_at(2 * m + 1)), m == 0, m == 3).then_inc(w_used, 1)
            for s in range(2):
                n = P_POOL + s
                half = wait_half(pe, f"po{s}")
                pe.wait_ge(pool_rdy, 4 * s + 4)
                pe.wait_ge(lo_done, n + 1)
                wh, wl = w_hi[n % SPLIT_SLOTS], w_lo[n % SPLIT_SLOTS]
                for b in range(4):
                    g, mt = divmod(b, 2)
                    for kt in range(2):
                        cs = slice(256 * kt + P * mt, 256 * kt + P * mt + P)
                        ins = three(ps[:, half, b, :], (wh[:, g, cs], wl[:, g, cs]), None,
                                    h_at(8 + 4 * s + 2 * g + kt), None, kt == 0, kt == 1)
                ins.then_inc(w_used, 1)
            for n in range(P_OUT, P_GATE):
                s, m = divmod(n - P_OUT, 8)
                half = jobs[f"wo{s}"][0]
                if m == 0:
                    wait_half(pe, f"wo{s}")
                if s == 0:
                    pe.wait_ge(*((ms_rdy, 2 * m + 2) if m < 4 else (mp_rdy, 2 * (m - 4) + 2)))
                pe.wait_ge(lo_done, n + 1)
                at_k = m_at if m < 4 else h_at
                weight_pair(n, half, (at_k(2 * (m % 4)), at_k(2 * (m % 4) + 1)), m == 0, False) \
                    .then_inc(w_used, 1)
                if m == 7:
                    pe.wait_ge(xa_loaded, 16 * CH)
                    for b in range(4):
                        for t in range(4):
                            ins = mm(ps[:, half, b, P * t:P * t + P],
                                     x_again[:, t, P * (4 * s + b):P * (4 * s + b) + P], ident[:, :],
                                     start=False, stop=t == 3)
                    ins.then_inc(aux_done, 1)

            def ffn_pair(n, half, m, lo=None):
                pe.wait_ge(lo_done, n + 1 if lo is None else lo)
                acts = [h_at((k + 8) % 16) for k in (2 * m, 2 * m + 1)]
                weight_pair(n, half, acts, m == 0, m == 7).then_inc(w_used, 1)

            def down_pair(n, half, kp, lo=None):
                pe.wait_ge(lo_done, n + 1 if lo is None else lo)
                wh, wl = w_hi[n % SPLIT_SLOTS], w_lo[n % SPLIT_SLOTS]
                for kt in range(2):
                    for t in range(4):
                        ts_ = slice(P * t, P * t + P)
                        k = 2 * kp + kt
                        ins = three(ps[:, half, t, :], (wh[:, kt, :], wl[:, kt, :]), None,
                                    (F_hi[:, k, ts_], F_lo[:, k, ts_]), None,
                                    k == 0, k == 3, stationary_is_w=False)
                ins.then_inc(w_used, 1)

            half = wait_half(pe, "gate")
            for m in range(8):
                pe.wait_ge(h_rdy, 2 * m + 2)
                ffn_pair(P_GATE + m, half, m)
            half = wait_half(pe, "rms2")
            pe.wait_ge(acc_rdy, 1)
            mm(ps[:, half, 0, :], ones[:, :], sqa[:, :], start=True, stop=True).then_inc(aux_done, 1)
            for t in range(4):
                half = wait_half(pe, f"tok{t}")
                for k in range(KT):
                    ins = nc.tensor.transpose(ps[:, half, k // 4, P * (k % 4):P * (k % 4) + P],
                                              resT[:, k, P * t:P * t + P], ident[:, :])
                ins.then_inc(aux_done, 1)
            half = wait_half(pe, "up")
            for m in range(8):
                ffn_pair(P_UP + m, half, m)
            with nc.tensor.Fori(0, FG - 1) as i:
                def lo(m):
                    return i * PER + (P_LOOP + m + 1)
                pe.wait_ge(*loop_free("gate", i, 0))
                for m in range(8):
                    ffn_pair(P_LOOP + m, LOOP["gate"][0], m, lo(m))
                pe.wait_ge(ff_rdy, i * 4 + 4)
                for c in range(4):
                    pe.wait_ge(*loop_free(f"down{c}", i, 0))
                    for kp in range(2):
                        down_pair(P_LOOP + 8 + 2 * c + kp, LOOP[f"down{c}"][0], kp, lo(8 + 2 * c + kp))
                pe.wait_ge(*loop_free("up", i, 0))
                for m in range(8):
                    ffn_pair(P_LOOP + 16 + m, LOOP["up"][0], m, lo(16 + m))
            pe.wait_ge(ff_rdy, 4 * FG)
            for c in range(4):
                half = c % 2
                if c < 2:
                    pe.wait_ge(free[half], loop_uses[half] + 3 * (FG - 1))
                else:
                    pe.wait_ge(fin_rdy, 4 * (c - 1))
                for kp in range(2):
                    down_pair(P_LAST + 2 * c + kp, half, kp)


_INS = ["x", "norm_mix", "w_in", "lambda_re", "lambda_im", "log_step", "b_re", "b_im", "c_re", "c_im",
        "d_skip", "w_glu", "b_glu", "w_pool", "b_pool", "pool_scale", "w_out", "norm_ffn", "w_gate",
        "w_up", "w_down", "norm_final"]


def kernel(**inputs):
    import numpy as np
    import concourse.bacc as bacc
    from concourse import mybir as mb
    from concourse.bass_utils import run_bass_kernel_spmd

    nc = bacc.Bacc("TRN2", target_bir_lowering=False, num_devices=1)
    arrays, args = {}, []
    for name in _INS:
        a = np.ascontiguousarray(inputs[name])
        arrays[f"in_{name}"] = a
        args.append(nc.dram_tensor(f"in_{name}", a.shape, mb.dt.from_np(a.dtype), kind="ExternalInput").ap())
    args.append(nc.dram_tensor("out_0", (1, SEQ, D_MODEL), mb.dt.float32, kind="ExternalOutput").ap())
    emit(nc, *args)
    r = run_bass_kernel_spmd(nc, [arrays], core_ids=[0])
    return r.results[0]["out_0"]
```

```python
import math
from contextlib import ExitStack

import concourse.bass as bass
from concourse import mybir

D_MODEL = 2048
SEQ = 512
SSM_WIDTH = 1024
GROUPS, STATE, GCH = 64, 64, 16
WINDOWS = (2, 4, 8, 16)
POOL_GROUP = 256
D_FF = ((8 * D_MODEL // 3 + 255) // 256) * 256
EPS = 1e-6

P = 128
KT = D_MODEL // P
NW = 512
CH = 8
NC = SEQ // CH
ROUNDS = 4
FG = D_FF // NW

RAW_SLOTS = 3
SPLIT_SLOTS = 3
LATE_SLOTS = 8 - SPLIT_SLOTS


def emit(nc, x, norm_mix, w_in, lambda_re, lambda_im, log_step, b_re, b_im, c_re, c_im, d_skip,
         w_glu, b_glu, w_pool, b_pool, pool_scale, w_out, norm_ffn, w_gate, w_up, w_down,
         norm_final, out):
    f32, f32r, i32 = mybir.dt.float32, mybir.dt.float32r, mybir.dt.int32
    ALU, ACT, AX = mybir.AluOpType, mybir.ActivationFunctionType, mybir.AxisListType
    mult, add, sub = ALU.mult, ALU.add, ALU.subtract

    base = (nc.sbuf_base + 63) // 64 * 64
    end = nc.sbuf_usable_end

    def at(name, shape, dt, offset):
        size = 4
        for n in shape[1:]:
            size *= n
        assert offset + size <= end, (name, offset, size, end)
        return nc.alloc_sbuf_tensor_at(name, shape, dt, offset=offset)

    KB = 1024
    R_H = base
    R_A = R_H + 64 * KB
    R_W = R_A + 32 * KB
    R_S = R_W + RAW_SLOTS * 4 * KB + SPLIT_SLOTS * 8 * KB

    H_hi = at("H_hi", [P, KT, SEQ], f32r, R_H)
    H_lo = at("H_lo", [P, KT, SEQ], f32r, R_H + 32 * KB)
    x_tok = at("x_tok", [P, 4, D_MODEL], f32, R_A)
    UG = at("UG", [P, 8, CH, NC], f32, R_A)
    V = at("V", [P, 8, CH, NC], f32, R_A + 16 * KB)
    res_tok = at("res_tok", [P, 4, D_MODEL], f32, R_A)
    raw = [at(f"raw{i}", [P, 2, NW], f32, R_W + 4 * KB * i) for i in range(RAW_SLOTS)]
    R_W2 = R_W + RAW_SLOTS * 4 * KB
    w_hi = [at(f"w_hi{i}", [P, 2, NW], f32r, R_W2 + 8 * KB * i) for i in range(SPLIT_SLOTS)]
    w_lo = [at(f"w_lo{i}", [P, 2, NW], f32r, R_W2 + 8 * KB * i + 4 * KB) for i in range(SPLIT_SLOTS)]

    top = [R_S]

    def take(name, shape, dt=f32, part=P):
        size = 4
        for n in shape:
            size *= n
        t = at(name, [part, *shape], dt, top[0])
        top[0] += (size + 31) // 32 * 32
        return t

    ident = take("ident", [P])
    ones = take("ones", [P])
    vecs = take("vecs", [P])
    rstd = take("rstd", [SEQ])
    ssq = take("ssq", [4, 4])
    rtok = take("rtok", [4])
    vtok = take("vtok", [4])
    stok = take("stok", [4])
    inv_n = take("inv_n", [2, CH])
    R_T = top[0]
    mask = take("mask", [8, GCH])
    bb_re = take("bb_re", [4, 8, GCH])
    bb_im = take("bb_im", [4, 8, GCH])
    ct_re = take("ct_re", [4, 8, GCH])
    ct_in = take("ct_in", [4, 8, GCH])
    lp_re = take("lp_re", [CH + 1, 32])
    lp_im = take("lp_im", [CH + 1, 32])
    par = take("par", [24, 32])
    pari = take("pari", [32], i32)
    ph_c = take("ph_c", [32, NC])
    ph_s = take("ph_s", [32, NC])
    R_Q = top[0]
    QR = [take(f"q{k}", [8, CH, GCH]) for k in ("re", "im")]
    zr = take("zr", [8, NC])
    zi = take("zi", [8, NC])
    zt = take("zt", [8, NC])
    BD = take("BD", [2, CH, P])
    Q2 = [at(f"q2{k}", [P, CH, 8, GCH], f32, top[0] - 8 * KB + 4 * KB * n)
          for n, k in enumerate(("re", "im"))]
    R_QT = top[0]
    QT = take("QT", [2, 8, P])
    U8 = take("U8", [2, 8, NC])
    s_re = take("s_re", [8, NC + 1])
    s_im = take("s_im", [8, NC + 1])
    yt = at("yt", [64, CH, 2, P], f32, R_QT)
    tmp1024 = at("tmp1024", [P, 8, CH, GCH], f32, R_Q + 8 * KB)
    c_raw = [at(f"c_raw{k}", [P, 8, STATE], f32, R_Q + 2 * KB * k) for k in range(2)]
    b_raw = [at(f"b_raw{k}", [P, 4, 8, GCH], f32, R_QT + 2 * KB * k) for k in range(2)]
    t512 = [at(f"t512_{k}", [P, 32, GCH], f32, R_Q + 4 * KB + 2 * KB * k) for k in range(2)]
    pw = [at(f"pw{k}", [P, 4, 32], f32, R_Q + 4 * KB + 512 * k) for k in range(2)]
    pt = [at(f"pt{k}", [P, 32, 32], f32, R_A + 16 * KB + 4 * KB * k) for k in range(2)]
    vec_rows = at("vec_rows", [P, P], f32, R_QT + 4 * KB)
    gain_rows = at("gain_rows", [KT, P], f32, R_QT + 6 * KB)
    lstep = at("lstep", [P, 4, 8], f32, R_QT + 5 * KB)
    sq_junk = at("sq_junk", [P, D_MODEL], f32, R_Q + 14 * KB)
    diag = at("diag", [P, 4, P], f32, R_Q + 8 * KB)


    M_hi = at("M_hi", [P, 8, SEQ], f32r, R_T)
    M_lo = at("M_lo", [P, 8, SEQ], f32r, R_T + 16 * KB)
    resT = at("resT", [P, KT, SEQ], f32, R_T + 32 * KB)
    gsig = at("gsig", [P, 4, SEQ], f32, R_T + 32 * KB)
    pmix = at("pmix", [P, 4, SEQ], f32, R_T + 40 * KB)
    sqt = at("sqt", [P, SEQ], f32, R_T + 64 * KB)
    sqa = at("sqa", [P, SEQ], f32, R_T + 66 * KB)
    assert top[0] <= R_T + 69 * KB
    top[0] = max(top[0], R_T + 68 * KB)
    pl = [take(f"pl{k}", [CH, NC]) for k in range(2)]
    pl_s = take("pl_s", [2, CH])
    dpl = [at(f"dpl{k}", [P, CH, NC], f32, R_Q + 8 * KB + 2 * KB * k) for k in range(2)]
    dpl_s = at("dpl_s", [P, 2, CH], f32, R_Q + 12 * KB)
    F_hi = at("F_hi", [P, 4, SEQ], f32r, R_T)
    F_lo = at("F_lo", [P, 4, SEQ], f32r, R_T + 8 * KB)
    gate = at("gate", [P, 4, SEQ], f32, R_T + 16 * KB)
    fsq = at("fsq", [P, NW], f32, R_H)
    gfin = at("gfin", [P, D_MODEL], f32, R_T + 24 * KB)
    late = [[at(f"late_{part}{m}", [P, 2, NW], f32r, R_T + (32 + 8 * m + 4 * k) * KB)
             for k, part in enumerate(("hi", "lo"))] for m in range(LATE_SLOTS)]
    assert R_T + (32 + 8 * LATE_SLOTS) * KB <= top[0]
    u_dram = nc.dram_tensor("u_dram", (8, P, CH, NC), f32).ap()

    ctx = ExitStack()
    with ctx:
        ps = ctx.enter_context(nc.psum_tensor("ps", [P, 2, 4, 512], f32))

        def sem(name):
            return ctx.enter_context(nc.semaphore(name))

        free = [sem("half0_free"), sem("half1_free")]
        x_loaded = [sem(f"x_loaded{i}") for i in range(4)]
        raw_full = [sem(f"raw_full{i}") for i in range(RAW_SLOTS)]
        hi_done = sem("w_hi_done")
        lo_done = sem("w_lo_done")
        w_used = sem("w_used")
        aux_done = sem("aux_done")
        gains_loaded = sem("gains_loaded")
        rows_loaded = sem("vector_rows_loaded")
        step_loaded = sem("log_step_loaded")
        b_loaded = sem("b_loaded")
        c_loaded = sem("c_loaded")
        u_stored = sem("u_stored")
        u8_loaded = sem("u8_loaded")
        gf_loaded = sem("final_gain_loaded")
        out_stored = sem("out_stored")
        consts = sem("consts_ready")
        x_hi = sem("x_hi")
        x_lo = sem("x_lo")
        x_sq = sem("x_squares")
        trig_in = sem("trig_in")
        trig = sem("trig")
        chain = sem("dve_chain")
        gp_chain = sem("gp_chain")
        var_rdy = sem("mean_square_ready")
        root_done = sem("root_done")
        diag_rdy = sem("diag_ready")
        q_rdy = sem("q_ready")
        q2_rdy = sem("q2_ready")
        r_rdy = sem("r_ready")
        bd_rdy = sem("bd_ready")
        s_cleared = sem("s_cleared")
        s_rdy = sem("s_ready")
        pooled = sem("pooled")
        pool_rdy = sem("pooled_split")
        g_rdy = sem("g_split")
        ms_rdy = sem("mixed_ssm_split")
        mp_rdy = sem("mixed_pool_split")
        h_rdy = sem("h_split")
        acc_rdy = sem("squares_ready")
        silu_done = sem("silu_done")
        scaled_rdy = sem("silu_scaled")
        ff_new = sem("ff_products")
        ff_hi = sem("ff_hi")
        ff_rdy = sem("ff_split")
        down_done = sem("last_down_done")
        fin_rdy = sem("final_tiles")
        fin_sq = sem("final_squares")
        o_rdy = sem("out_rows")

        jobs = {}
        uses = [0, 0]

        def job(name, half):
            jobs[name] = (half, uses[half], uses[half] + 1)
            uses[half] += 1

        P_GLU, P_POOL, P_OUT, P_GATE, P_UP, P_LOOP = 32, 40, 42, 74, 82, 90
        PER = 24
        P_LAST = P_LOOP + PER * (FG - 1)
        assert PER % RAW_SLOTS == 0 and PER % SPLIT_SLOTS == 0
        IN_COLS = (0, 1, 3, 2)
        after = {0: [("xt", 1)], 1: [("vec", 0)], 2: [("xt", 2)], 3: [("xt", 3)], 4: [("ct", 0)],
                 5: [("rms", 0)]}
        for r in range(ROUNDS):
            for kind, d in (("a", 0), ("b", 1), ("e", 2), ("i", 5), ("y", 6)):
                after.setdefault(9 + 6 * r + d, []).append((kind, r))
        for p in after:
            after[p].sort(key=lambda job_: job_[0] == "a")
        for t in range(4):
            after[P_GATE + 1 + t] = [("tok", t)]
        after[P_GATE + 5] = [("rms2", 0)]

        def key(kind, r):
            return f"{kind}{r}" if kind in ("xt", "tok") or kind in "abeiy" else kind

        job("gains", 0)
        job("xt0", 0)
        aux_order = ["gains", "xt0"]
        products = ([("in", s, 8) for s in range(4)] + [("gl", s, 4) for s in range(2)]
                    + [("po", s, 1) for s in range(2)] + [("wo", s, 8) for s in range(4)]
                    + [("gate", None, 8), ("up", None, 8)])
        n = 0
        for number, (name, s, pairs) in enumerate(products):
            half = (number + 1) % 2
            job(name if s is None else f"{name}{s}", half)
            for p in range(n, n + pairs):
                for kind, r in after.get(p, []):
                    job(key(kind, r), 1 - half)
                    aux_order.append(key(kind, r))
            n += pairs
            if name == "wo":
                aux_order.append(f"wo{s}")
        aux_count = {name: n + 1 for n, name in enumerate(aux_order)}
        loop_uses = tuple(uses)
        G = jobs["gate"][0]
        LOOP = {"gate": (G, 0), "down0": (1 - G, 0), "down1": (G, 1), "down2": (1 - G, 1),
                "down3": (G, 2), "up": (1 - G, 2)}
        assert jobs["up"][0] == 1 - G
        LAST_HALF = (G, 1 - G, G, 1 - G)
        def split_slot(n):
            m = n - P_LAST
            if 0 <= m < LATE_SLOTS:
                return late[m]
            slot = (m - LATE_SLOTS if m >= 0 else n) % SPLIT_SLOTS
            return w_hi[slot], w_lo[slot]

        def slot_used(n):
            m = n - P_LAST
            if n < SPLIT_SLOTS or 0 <= m < LATE_SLOTS:
                return None
            return n - SPLIT_SLOTS + 1 - (LATE_SLOTS if m >= 0 else 0)

        def wait_half(eng, name):
            half, need, _ = jobs[name]
            if need:
                eng.wait_ge(free[half], need)
            return half

        def wait_emptied(eng, name):
            half, _, then = jobs[name]
            eng.wait_ge(free[half], then)

        def wait_aux(eng, name):
            eng.wait_ge(aux_done, aux_count[name])

        def loop_free(name, i, after):
            half, nth = LOOP[name]
            return free[half], i * 3 + (loop_uses[half] + nth + after)

        def pair_src(w, rows, cols):
            return w[0, rows:rows + 2 * P, cols].rearrange("(k p) n -> p k n", p=P)

        def static_src(n):
            def cols(s):
                return slice(s * NW, (s + 1) * NW)
            if n < P_GLU:
                return pair_src(w_in, 256 * (n % 8), cols(IN_COLS[n // 8]))
            if n < P_POOL:
                s, m = divmod(n - P_GLU, 4)
                return pair_src(w_glu, 256 * m, cols(s))
            if n < P_OUT:
                m = n - P_POOL
                return w_pool[0, 2 * m:2 * m + 2, :, :].rearrange("g (k p) d -> p g k d", p=P)
            if n < P_GATE:
                s, m = divmod(n - P_OUT, 8)
                return pair_src(w_out, 256 * m, cols(s))
            if n < P_UP:
                return pair_src(w_gate, 256 * (n - P_GATE), cols(0))
            return pair_src(w_up, 256 * (n - P_UP), cols(0))

        def levels(k):
            return WINDOWS[k // 2].bit_length() - 1

        def level_sums(sums, k, level):
            return V[:, k, :, :] if level == 0 else sums[level % 2][:, :, :]

        def shifted_add(engine, step, settle, sums, k, level):
            s, a, o = 2 ** level, level_sums(sums, k, level), level_sums(sums, k, level + 1)
            if s < CH:
                step(engine.tensor_tensor(o[:, s:, :], a[:, s:, :], a[:, :CH - s, :], add))
                step(engine.tensor_tensor(o[:, 0:s, 1:], a[:, 0:s, 1:], a[:, CH - s:, :NC - 1], add))
                step(engine.tensor_copy(o[:, 0:s, 0:1], a[:, 0:s, 0:1]))
            else:
                step(engine.tensor_tensor(o[:, :, 1:], a[:, :, 1:], a[:, :, :NC - 1], add))
                step(engine.tensor_copy(o[:, :, 0:1], a[:, :, 0:1]))
            settle()

        def window_mean(engine, step, settle, sums, head, k):
            w, v, cur = WINDOWS[k // 2], V[:, k, :, :], level_sums(sums, k, levels(k))
            nj, ncol = min(w, CH), max(1, w // CH)
            for c in range(ncol):
                step(engine.tensor_tensor(head[:, c, 0:nj], cur[:, 0:nj, c], inv_n[:, c, 0:nj], mult))
            settle()
            for c in range(ncol):
                step(engine.tensor_tensor(head[:, c, 0:nj], head[:, c, 0:nj], v[:, 0:nj, c], sub))
            if engine is nc.vector:
                settle()
                step(engine.scalar_tensor_tensor(out=v, in0=cur, scalar=1.0 / w, in1=v,
                                                 op0=mult, op1=sub))
            else:
                step(engine.tensor_scalar(cur, cur, 1.0 / w, None, mult))
                settle()
                step(engine.tensor_tensor(v, cur, v, sub))
            settle()
            for c in range(ncol):
                ins = engine.tensor_copy(v[:, 0:nj, c], head[:, c, 0:nj])
                if c < ncol - 1:
                    step(ins)
            return ins

        block = ctx.enter_context(nc.Block())

        @block.sync
        def _(sp):
            def load(n, src, done=None):
                if n >= RAW_SLOTS:
                    sp.wait_ge(lo_done, n - RAW_SLOTS + 1 if done is None else done)
                dst = raw[n % RAW_SLOTS][:, :, :]
                if P_POOL <= n < P_OUT:
                    dst = dst.rearrange("p g (k d) -> p g k d", k=2)
                sp.dma_start(dst, src).then_inc(raw_full[n % RAW_SLOTS], 16)

            def load_x(s):
                for j in range(2):
                    sp.dma_start(x_tok[64 * j:64 * j + 64, :, NW * s:NW * s + NW],
                                 x[0].rearrange("(c t j) n -> j c t n", t=4, j=2)
                                 [j, :, :, NW * s:NW * s + NW]).then_inc(x_loaded[s], 16)

            def rows(v):
                return v.rearrange("o (r p) -> (o r) p", p=P)

            def load_vectors():
                for q in range(2):
                    sp.dma_start(lstep[64 * q:64 * q + 64, :, :],
                                  log_step[0].rearrange("(b q g) -> q b g", q=2, g=8)[q]
                                  .partition_broadcast(64)).then_inc(step_loaded, 16)
                for k, lam in enumerate((lambda_re, lambda_im)):
                    for b in range(4):
                        r0 = 64 + 32 * k + 8 * b
                        sp.dma_start(vec_rows[r0:r0 + 8, :].rearrange("g (q p) -> g q p", q=2),
                                      lam[0, 16 * b:16 * b + 16, :]
                                      .rearrange("(q g) p -> g q p", q=2)).then_inc(rows_loaded, 16)
                for src, r0, n in ((rows(norm_mix), 0, 16), (rows(norm_ffn), 16, 16),
                                   (rows(b_glu), 32, 8),
                                   (b_pool.rearrange("o k (r p) -> (o k r) p", p=P), 40, 8),
                                   (rows(pool_scale), 48, 8),
                                   (d_skip.rearrange("o (r g) h -> (o r) (g h)", g=8), 56, 8)):
                    sp.dma_start(vec_rows[r0:r0 + n, :], src).then_inc(rows_loaded, 16)

            def load_c():
                for k, cm in enumerate((c_re, c_im)):
                    sp.dma_start(c_raw[k][:, :, :],
                                  cm[0].rearrange("(b g) h p -> (g h) b p", g=8)).then_inc(c_loaded, 16)

            def load_b(q):
                for k, bm in enumerate((b_re, b_im)):
                    for b in range(4):
                        sp.dma_start(b_raw[k][64 * q:64 * q + 64, b, :, :],
                                     bm[0, 16 * b + 8 * q:16 * b + 8 * q + 8, :, :]
                                     .rearrange("g p h -> p g h")).then_inc(b_loaded, 16)

            for s in range(4):
                load_x(s)
                if s < RAW_SLOTS:
                    load(s, static_src(s))
            load_vectors()

            def store_u(r):
                wait_emptied(sp, f"in{r // 2}")
                sp.dma_start(u_dram[2 * r:2 * r + 2].rearrange("b p k c -> p b k c"),
                             UG[:, 2 * r:2 * r + 2, :, :]).then_inc(u_stored, 16)

            def load_u8(r):
                sp.wait_ge(u_stored, 32 * (r // 2 + 1))
                if r:
                    wait_aux(sp, f"e{r - 1}")
                for d in range(CH):
                    sp.dma_start(U8[16 * d:16 * d + 16, :, :, :],
                                 u_dram[2 * r:2 * r + 2, :, CH - 1 - d, :]
                                 .rearrange("q (g h) c -> h q g c", h=GCH)).then_inc(u8_loaded, 16)

            store_at = {13: (0, 1), 21: (2, 3)}
            u8_at = {13: 0, 17: 1, 23: 2, 29: 3}
            for n in range(RAW_SLOTS, P_LOOP):
                load(n, static_src(n))
                if n == 3:
                    load_c()
                if n in (4, 5):
                    load_b(n - 4)
                for r in store_at.get(n, ()):
                    store_u(r)
                if n in u8_at:
                    load_u8(u8_at[n])
                if P_OUT + 6 <= n < P_OUT + 10:
                    if n == P_OUT + 6:
                        sp.wait_ge(ms_rdy, 8)
                        sp.wait_ge(pool_rdy, 8)
                    load_x(n - (P_OUT + 6))

            with nc.sync.Fori(0, FG - 1) as i:
                for m in range(PER):
                    if m < 8:
                        src = w_gate[0, 256 * m:256 * m + 256, bass.ds(i * NW + NW, NW)]
                    elif m < 16:
                        c, kp = divmod(m - 8, 2)
                        src = w_down[0, bass.ds(i * NW + 256 * kp, 256), c * NW:(c + 1) * NW]
                    else:
                        src = w_up[0, 256 * (m - 16):256 * (m - 16) + 256, bass.ds(i * NW + NW, NW)]
                    load(P_LOOP + m, src.rearrange("(k p) n -> p k n", p=P),
                         done=i * PER + (P_LOOP + m - RAW_SLOTS + 1))
            for m in range(8):
                c, kp = divmod(m, 2)
                load(P_LAST + m, pair_src(w_down, (FG - 1) * NW + 256 * kp, slice(c * NW, (c + 1) * NW)))
            sp.dma_start(gfin[:, :], norm_final.partition_broadcast(P)).then_inc(gf_loaded, 16)
            for t in range(4):
                for part in range(2):
                    cs = slice(2 * NW * part, 2 * NW * (part + 1))
                    sp.wait_ge(o_rdy, 2 * t + part + 1)
                    for j in range(2):
                        sp.dma_start(out[0, 2 * t + j:SEQ:CH, cs], res_tok[64 * j:64 * j + 64, t, cs]) \
                            .then_inc(out_stored, 16)
            sp.wait_ge(out_stored, 16 * 16)

        @block.scalar
        def _(act):
            def round_hi(n, full=None, used=None):
                act.wait_ge(raw_full[n % RAW_SLOTS], 16 * (n // RAW_SLOTS + 1) if full is None else full)
                used = slot_used(n) if used is None else used
                if used is not None:
                    act.wait_ge(w_used, used)
                nc.scalar.copy(split_slot(n)[0][:, :, :], raw[n % RAW_SLOTS][:, :, :]).then_inc(hi_done, 1)

            def x_tiles(s):
                wait_aux(act, f"xt{s}")
                half = jobs[f"xt{s}"][0]
                for b in range(4):
                    k = 4 * s + b
                    nc.scalar.activation(H_hi[:, k, :], ps[:, half, b, :], ACT.Copy,
                                         scale=vecs[:, k:k + 1]).then_inc(x_hi, 1)

            def x_square(t):
                if t:
                    act.wait_ge(x_sq, t)
                nc.scalar.activation(sq_junk[:, :], x_tok[:, t, :], ACT.Square,
                                     accum_out=ssq[:, t, 0:1]).then_inc(x_sq, 1)

            act.dma_start(gain_rows[:, :], norm_mix.rearrange("o (r p) -> (o r) p", p=P)) \
                .then_inc(gains_loaded, 16)
            round_hi(0)
            wait_emptied(act, "gains")
            x_tiles(0)
            round_hi(1)
            x_tiles(1)
            round_hi(2)
            for s in range(4):
                act.wait_ge(x_loaded[s], 32)
            x_square(0)
            x_square(1)
            round_hi(3)
            x_square(2)
            x_square(3)
            x_tiles(2)
            round_hi(4)
            act.wait_ge(trig_in, 1)
            nc.scalar.activation(par[:, 8, :], par[:, 6, :], ACT.Sin).then_inc(trig, 1)
            nc.scalar.activation(par[:, 9, :], par[:, 7, :], ACT.Sin).then_inc(trig, 1)
            act.wait_ge(var_rdy, 1)
            nc.scalar.activation(stok[:, :], vtok[:, :], ACT.Sqrt).then_inc(root_done, 1)
            round_hi(5)
            x_tiles(3)

            def small(kind, r):
                half = jobs[key(kind, r)][0]
                if kind == "a":
                    wait_aux(act, f"a{r}")
                    for b in range(4):
                        last = nc.scalar.copy(
                            QT[:, b // 2, 4 * (b % 2):4 * (b % 2) + 4, :],
                            ps[:, half, b, :].rearrange("p (g q) -> p g q", g=4))
                    last.then_inc(free[half], 1)
                elif kind == "e":
                    wait_aux(act, f"e{r}")
                    act.wait_ge(s_cleared, 2)
                    if r:
                        act.wait_ge(s_rdy, r)
                    for k, st in enumerate((s_re, s_im)):
                        last = nc.scalar.copy(st[:, :, 1:],
                                              ps[:, half, k, :].rearrange("p (g c) -> p g c", g=8))
                    last.then_inc(free[half], 1)
                elif kind == "i":
                    wait_aux(act, f"i{r}")
                    for b in range(4):
                        last = nc.scalar.copy(
                            yt[:, :, b // 2, 64 * (b % 2):64 * (b % 2) + 64]
                            .rearrange("c j (g h) -> c g j h", h=GCH),
                            ps[0:64, half, b, :].rearrange("c (g j h) -> c g j h", g=4, h=GCH))
                    last.then_inc(free[half], 1)
                elif kind == "y":
                    wait_aux(act, f"y{r}")
                    for q in range(2):
                        last = nc.scalar.activation(
                            UG[:, 2 * r + q, :, :], ps[:, half, q, :].rearrange("p (j c) -> p j c", j=CH),
                            ACT.Gelu)
                    last.then_inc(free[half], 1)
                elif kind == "tok":
                    wait_aux(act, f"tok{r}")
                    for b in range(4):
                        last = nc.scalar.copy(res_tok[:, r, NW * b:NW * b + NW], ps[:, half, b, :])
                    last.then_inc(free[half], 1)
                elif kind == "rms2":
                    act.wait_ge(var_rdy, 2)
                    nc.scalar.activation(sqt[:, :], sqa[:, :], ACT.Sqrt).then_inc(root_done, 1)

            for n in range(6, P_LOOP):
                round_hi(n)
                behind = n - SPLIT_SLOTS
                for kind, r in after.get(behind, []):
                    small(kind, r)
                for s in range(2):
                    if behind == P_GLU + 4 * s + 3:
                        act.wait_ge(w_used, behind + 1)
                        half = jobs[f"gl{s}"][0]
                        if s:
                            act.wait_ge(ms_rdy, 4)
                        for b in range(4):
                            last = nc.scalar.activation(gsig[:, b, :], ps[:, half, b, :], ACT.Sigmoid,
                                                        bias=vecs[:, 32 + 4 * s + b:33 + 4 * s + b])
                        last.then_inc(free[half], 1)
                if behind == P_GATE + 7:
                    wait_emptied(act, "gate")
                    for b in range(4):
                        nc.scalar.activation(gate[:, b, :], gate[:, b, :], ACT.Silu).then_inc(silu_done, 1)

            with nc.scalar.Fori(0, FG - 1) as i:
                for m in range(PER):
                    n = P_LOOP + m
                    round_hi(n, full=i * (16 * PER // RAW_SLOTS) + 16 * (n // RAW_SLOTS + 1),
                             used=i * PER + (n - SPLIT_SLOTS + 1))
                    if m == 7 + SPLIT_SLOTS:
                        act.wait_ge(*loop_free("gate", i, 1))
                        for b in range(4):
                            nc.scalar.activation(gate[:, b, :], gate[:, b, :], ACT.Silu) \
                                .then_inc(silu_done, 1)
            for m in range(8):
                round_hi(P_LAST + m)
            for t in range(4):
                for c in range(4):
                    m = 4 * t + c
                    act.wait_ge(fin_rdy, m + 1)
                    if m:
                        act.wait_ge(fin_sq, m)
                    nc.scalar.activation(fsq[:, :], res_tok[:, t, NW * c:NW * c + NW], ACT.Square,
                                         accum_out=ssq[:, t, c:c + 1]).then_inc(fin_sq, 1)
                act.wait_ge(var_rdy, 3 + t)
                nc.scalar.activation(stok[:, t:t + 1], vtok[:, t:t + 1], ACT.Sqrt).then_inc(root_done, 1)

        @block.gpsimd
        def _(gp):
            nc.gpsimd.memset(ident[:, :], 0.0).then_inc(consts, 1)
            nc.gpsimd.memset(ones[:, :], 1.0).then_inc(consts, 1)
            nc.gpsimd.memset(mask[:, :, :], 1.0).then_inc(consts, 1)
            gp.wait_ge(consts, 3)
            nc.gpsimd.affine_select(out=ident[:, :], in_=ident[:, :], compare_op=ALU.not_equal, fill=1.0,
                                    base=0, pattern=[[-1, P]], channel_multiplier=1).then_inc(consts, 1)
            nc.gpsimd.affine_select(out=mask[:, :, :], in_=mask[:, :, :], compare_op=ALU.is_ge, fill=0.0,
                                    base=0, pattern=[[-GCH, 8], [0, GCH]], channel_multiplier=1) \
                .then_inc(consts, 1)
            gp.wait_ge(consts, 5)
            nc.gpsimd.affine_select(out=mask[:, :, :], in_=mask[:, :, :], compare_op=ALU.is_ge, fill=0.0,
                                    base=GCH - 1, pattern=[[GCH, 8], [0, GCH]], channel_multiplier=-1) \
                .then_inc(consts, 1)
            for c in range(2):
                for j in range(CH):
                    nc.gpsimd.memset(inv_n[:, c, j:j + 1], 1.0 / (CH * c + j + 1)).then_inc(consts, 1)
            ALL_CONSTS = 6 + 2 * CH

            def rest_lo(n, done=None):
                gp.wait_ge(hi_done, n + 1 if done is None else done)
                hi, lo = split_slot(n)
                nc.gpsimd.tensor_tensor(lo[:, :, :], raw[n % RAW_SLOTS][:, :, :],
                                        hi[:, :, :].bitcast(f32), sub).then_inc(lo_done, 1)

            steps = [0]

            def step(ins):
                steps[0] += 1
                ins.then_inc(gp_chain, 1)

            def settle():
                gp.wait_ge(gp_chain, steps[0])

            pieces = [(k, level) for k in range(4, 8) for level in range(levels(k) + 1)]
            gp.wait_ge(consts, ALL_CONSTS)
            for n in range(P_LOOP):
                rest_lo(n)
                if n < 26:
                    continue
                if n == 26:
                    wait_emptied(gp, "in2")
                for k, level in pieces[:2]:
                    pieces.pop(0)
                    if level < levels(k):
                        shifted_add(nc.gpsimd, step, settle, pl, k, level)
                    else:
                        window_mean(nc.gpsimd, step, settle, pl, pl_s, k).then_inc(pooled, 1)
                        gp.wait_ge(pooled, k - 3)
                        break
            with nc.gpsimd.Fori(0, FG - 1) as i:
                for m in range(PER):
                    rest_lo(P_LOOP + m, i * PER + (P_LOOP + m + 1))
            for m in range(8):
                rest_lo(P_LAST + m)

        @block.vector
        def _(dve):
            steps = [0]

            def step(ins):
                steps[0] += 1
                ins.then_inc(chain, 1)

            def settle():
                dve.wait_ge(chain, steps[0])

            def tt(o, a, b, op):
                step(nc.vector.tensor_tensor(o, a, b, op))

            def ts(o, a, s1, s2, op0, op1=None):
                if op1 is None:
                    step(nc.vector.tensor_scalar(o, a, s1, None, op0))
                else:
                    step(nc.vector.tensor_scalar(o, a, s1, s2, op0, op1))

            def stt(o, a, s, b, op0, op1):
                step(nc.vector.scalar_tensor_tensor(out=o, in0=a, scalar=s, in1=b, op0=op0, op1=op1))

            def inverse_root(y, var, root, nth):
                dve.wait_ge(root_done, nth)
                step(nc.vector.reciprocal(y, root))
                settle()
                tt(root, y, y, mult)
                settle()
                tt(root, root, var, mult)
                settle()
                ts(root, root, -0.5, 1.5, mult, add)
                settle()
                tt(y, y, root, mult)
                settle()

            wait_aux(dve, "gains")
            half = jobs["gains"][0]
            nc.vector.tensor_copy(vecs[:, 0:KT], ps[:, half, 0, 0:KT]).then_inc(free[half], 1)
            wait_emptied(dve, "gains")
            def x_tiles(s):
                wait_aux(dve, f"xt{s}")
                half = jobs[f"xt{s}"][0]
                for b in range(4):
                    k = 4 * s + b
                    dve.wait_ge(x_hi, k + 1)
                    last = nc.vector.scalar_tensor_tensor(
                        out=H_lo[:, k, :], in0=ps[:, half, b, :], scalar=vecs[:, k:k + 1],
                        in1=H_hi[:, k, :].bitcast(f32), op0=mult, op1=sub)
                    if b == 1:
                        last.then_inc(x_lo, 1)
                last.then_inc(free[half], 1)
            x_tiles(0)
            x_tiles(1)
            wait_aux(dve, "vec")
            half = jobs["vec"][0]
            nc.vector.tensor_copy(vecs[:, KT:P], ps[:, half, 0, KT:P]).then_inc(free[half], 1)
            wait_emptied(dve, "vec")

            lr, li = vecs[:, 64:96], vecs[:, 96:128]
            v_ = [par[:, k, :] for k in range(24)]
            LOG2E, MAGIC = 1.0 / math.log(2.0), 1.5 * 2.0 ** 23
            LN2_HI = 0.693145751953125
            LN2_LO = math.log(2.0) - LN2_HI

            def exp_parts(src, two_n, f, em1):
                ts(f, src, -88.0, 88.0, ALU.max, ALU.min)
                settle()
                ts(two_n, f, LOG2E, MAGIC, mult, add)
                settle()
                ts(two_n, two_n, MAGIC, None, sub)
                settle()
                stt(f, two_n, -LN2_HI, f, mult, add)
                settle()
                stt(f, two_n, -LN2_LO, f, mult, add)
                settle()
                ts(em1, f, 1.0 / 5040, None, mult)
                for c in (720, 120, 24, 6, 2, 1):
                    settle()
                    stt(em1, em1, 1.0 / c, f, add, mult)
                ts(pari[:, :], two_n, 127.0, 2.0 ** 23, add, mult)
                settle()
                step(nc.vector.tensor_copy(two_n, pari[:, :].bitcast(f32)))
                settle()

            dve.wait_ge(step_loaded, 32)
            exp_parts(lstep[:, :, :].rearrange("p b g -> p (b g)"), v_[0], v_[1], v_[2])
            tt(v_[3], v_[2], v_[0], mult)
            settle()
            tt(v_[3], v_[3], v_[0], add)
            settle()
            tt(v_[4], lr, v_[3], mult)
            tt(v_[5], li, v_[3], mult)
            settle()
            ts(v_[0], v_[5], 1.0 / (2 * math.pi), MAGIC, mult, add)
            settle()
            ts(v_[0], v_[0], MAGIC, None, sub)
            settle()
            c1, c2 = 6.28125, 0.00193500518798828125
            for c in (c1, c2, 2 * math.pi - c1 - c2):
                stt(v_[5], v_[0], -c, v_[5], mult, add)
                settle()
            ts(v_[6], v_[5], 0.5, None, mult)
            settle()
            ts(v_[6], v_[6], -math.pi / 2, math.pi / 2, ALU.max, ALU.min)
            settle()
            ts(v_[7], v_[6], -1.0, None, mult)
            settle()
            tt(v_[7], v_[7], v_[6], ALU.min)
            settle()
            nc.vector.tensor_scalar(v_[7], v_[7], math.pi / 2, None, add).then_inc(trig_in, 1)
            dve.wait_ge(x_sq, 4)
            nc.vector.tensor_scalar(vtok[:, :], ssq[:, :, 0], 1.0 / D_MODEL, EPS, mult, add) \
                .then_inc(var_rdy, 1)
            x_tiles(2)
            exp_parts(v_[4], v_[0], v_[1], v_[2])
            inverse_root(rtok[:, :], vtok[:, :], stok[:, :], 1)
            dve.wait_ge(consts, 6)
            for t in range(4):
                nc.vector.tensor_scalar(diag[:, t, :], ident[:, :], rtok[:, t:t + 1], None, mult) \
                    .then_inc(diag_rdy, 1)
            x_tiles(3)
            wait_aux(dve, "ct")
            half = jobs["ct"][0]
            step(nc.vector.tensor_copy(ct_re[:, :, :, :].rearrange("p b g h -> p (b g h)"),
                                       ps[:, half, 0, :]))
            nc.vector.tensor_scalar(ct_in[:, :, :, :].rearrange("p b g h -> p (b g h)"),
                                    ps[:, half, 1, :], -1.0, None, mult).then_inc(free[half], 1)
            wait_emptied(dve, "ct")
            tt(v_[11], v_[2], v_[0], mult)
            settle()
            tt(v_[10], v_[11], v_[0], add)
            stt(v_[11], v_[0], -1.0, v_[11], add, add)
            dve.wait_ge(trig, 2)
            tt(v_[12], v_[8], v_[9], mult)
            tt(v_[13], v_[8], v_[8], mult)
            settle()
            ts(v_[12], v_[12], 2.0, None, mult)
            ts(v_[14], v_[13], -2.0, 1.0, mult, add)
            settle()
            ts(v_[13], v_[13], -2.0, None, mult)
            step(nc.vector.memset(lp_re[:, 0, :], 1.0))
            step(nc.vector.memset(lp_im[:, 0, :], 0.0))
            tt(lp_re[:, 1, :], v_[10], v_[14], mult)
            tt(lp_im[:, 1, :], v_[10], v_[12], mult)
            tt(v_[15], v_[11], v_[14], mult)
            tt(v_[16], lr, lr, mult)
            tt(v_[17], li, li, mult)
            settle()
            tt(v_[15], v_[15], v_[13], add)
            tt(v_[16], v_[16], v_[17], add)
            settle()
            step(nc.vector.reciprocal(v_[21], v_[16]))
            tt(v_[17], v_[15], lr, mult)
            tt(v_[18], lp_im[:, 1, :], li, mult)
            tt(v_[19], lp_im[:, 1, :], lr, mult)
            tt(v_[20], v_[15], li, mult)
            settle()
            tt(v_[17], v_[17], v_[18], add)
            tt(v_[19], v_[19], v_[20], sub)
            settle()
            tt(v_[17], v_[17], v_[21], mult)
            tt(v_[19], v_[19], v_[21], mult)
            settle()

            def cmul(o, a, b, t1, t2):
                tt(o[0], a[0], b[0], mult)
                tt(t1, a[1], b[1], mult)
                tt(o[1], a[0], b[1], mult)
                tt(t2, a[1], b[0], mult)
                settle()
                tt(o[0], o[0], t1, sub)
                tt(o[1], o[1], t2, add)
                settle()

            def cols(v, n):
                return v.unsqueeze(2).to_broadcast([P, 32, n])

            def by_state(t):
                return t[:, :, :, :].rearrange("p b g h -> p (b g) h")

            dve.wait_ge(b_loaded, 16 * 16)
            cmul((by_state(bb_re), by_state(bb_im)), (cols(v_[17], GCH), cols(v_[19], GCH)),
                 (by_state(b_raw[0]), by_state(b_raw[1])), t512[0][:, :, :], t512[1][:, :, :])
            for first, n, by in ((2, 1, 1), (3, 2, 2), (5, 4, 4)):
                fac = [t[:, by, :].unsqueeze(1).to_broadcast([P, n, 32]) for t in (lp_re, lp_im)]
                cmul((lp_re[:, first:first + n, :], lp_im[:, first:first + n, :]),
                     (lp_re[:, 1:1 + n, :], lp_im[:, 1:1 + n, :]), fac,
                     pw[0][:, 0:n, :], pw[1][:, 0:n, :])

            wait_aux(dve, "rms")
            half = jobs["rms"][0]
            nc.vector.tensor_copy(rstd[:, :], ps[:, half, 0, :]).then_inc(free[half], 1)
            wait_emptied(dve, "rms")

            shape4 = [P, 8, CH, GCH]
            tmp = tmp1024[:, :, :, :]
            Q_re, Q_im = QR[0][:, :, :, :], QR[1][:, :, :, :]

            def power(t, first, r):
                return t[:, first:first + CH, 8 * r:8 * r + 8].rearrange("p d g -> p g d") \
                    .unsqueeze(3).to_broadcast(shape4)

            def chan(t, r):
                return t[:, r, :, :].unsqueeze(2).to_broadcast(shape4)

            def build_q(r):
                if r:
                    wait_aux(dve, f"i{r - 1}")
                tt(Q_re, power(lp_re, 0, r), chan(bb_re, r), mult)
                tt(tmp, power(lp_im, 0, r), chan(bb_im, r), mult)
                settle()
                tt(Q_re, Q_re, tmp, sub)
                tt(Q_im, power(lp_re, 0, r), chan(bb_im, r), mult)
                settle()
                tt(tmp, power(lp_im, 0, r), chan(bb_re, r), mult)
                settle()
                nc.vector.tensor_tensor(Q_im, Q_im, tmp, add).then_inc(q_rdy, 1)
                dve.wait_ge(q_rdy, r + 1)
                if r:
                    wait_aux(dve, f"y{r - 1}")
                for k in range(2):
                    nc.vector.tensor_copy(Q2[k][:, :, :, :].rearrange("p d g h -> p g d h"),
                                          QR[k][:, :, :, :]).then_inc(q2_rdy, 1)

            def build_r(r):
                wait_aux(dve, f"b{r}")
                tt(Q_re, power(lp_re, 1, r), chan(ct_re, r), mult)
                tt(tmp, power(lp_im, 1, r), chan(ct_in, r), mult)
                settle()
                tt(Q_re, Q_re, tmp, add)
                tt(Q_im, power(lp_re, 1, r), chan(ct_in, r), mult)
                settle()
                tt(tmp, power(lp_im, 1, r), chan(ct_re, r), mult)
                settle()
                nc.vector.tensor_tensor(Q_im, Q_im, tmp, sub).then_inc(r_rdy, 1)
                dve.wait_ge(r_rdy, r + 1)

            def taps(r):
                wait_aux(dve, f"b{r}")
                half = jobs[f"b{r}"][0]
                mk = mask[:, :, :].rearrange("p g h -> p (g h)").unsqueeze(1).to_broadcast([P, 4, P])
                for b in range(4):
                    ins = nc.vector.tensor_tensor(
                        BD[:, b // 2, 4 * (b % 2):4 * (b % 2) + 4, :],
                        ps[:, half, b, :].rearrange("p (d m) -> p d m", d=4), mk, mult)
                    if b < 3:
                        step(ins)
                ins.then_inc(free[half], 1)
                settle()
                for q in range(2):
                    k = 56 + 2 * r + q
                    nc.vector.scalar_tensor_tensor(out=BD[:, q, 0, :], in0=ident[:, :],
                                                   scalar=vecs[:, k:k + 1], in1=BD[:, q, 0, :],
                                                   op0=mult, op1=add).then_inc(bd_rdy, 1)

            def states(r):
                wait_emptied(dve, f"e{r}")
                pc, pn = ph_c[:, 8 * r:8 * r + 8, :], ph_s[:, 8 * r:8 * r + 8, :]
                ZR, ZI, ZT = zr[:, :, :], zi[:, :, :], zt[:, :, :]
                S_re, S_im = s_re[:, :, 1:], s_im[:, :, 1:]
                tt(ZR, S_re, pc, mult)
                tt(ZT, S_im, pn, mult)
                settle()
                tt(ZR, ZR, ZT, add)
                tt(ZI, S_im, pc, mult)
                settle()
                tt(ZT, S_re, pn, mult)
                settle()
                tt(ZI, ZI, ZT, sub)
                settle()
                for z in (zr, zi):
                    for g in range(8):
                        rho = v_[10][:, 8 * r + g:8 * r + g + 1].to_broadcast([P, NC])
                        step(nc.vector.tensor_tensor_scan(z[:, g, :], rho, z[:, g, :], 0.0, mult, add))
                settle()
                tt(S_re, ZR, pc, mult)
                tt(ZT, ZI, pn, mult)
                settle()
                tt(S_re, S_re, ZT, sub)
                tt(S_im, ZI, pc, mult)
                settle()
                tt(ZT, ZR, pn, mult)
                settle()
                nc.vector.tensor_tensor(S_im, S_im, ZT, add).then_inc(s_rdy, 1)
                dve.wait_ge(s_rdy, r + 1)

            def small(kind, r):
                if kind == "a" and r == ROUNDS - 1:
                    for k in range(4):
                        split_g(k)
                elif kind == "b":
                    taps(r)
                elif kind == "e":
                    build_r(r)
                    states(r)
                elif kind == "i" and r + 1 < ROUNDS:
                    build_q(r + 1)

            def split_tile(src, hi, lo, done):
                step(nc.vector.tensor_copy(hi, src))
                settle()
                nc.vector.tensor_tensor(lo, src, hi.bitcast(f32), sub).then_inc(done, 1)

            def projection(s):
                dve.wait_ge(w_used, 8 * s + 8)
                half, first = jobs[f"in{s}"][0], 4 * IN_COLS[s]
                for b in range(4):
                    dst = (UG, V)[first // 8][:, first % 8 + b, :, :]
                    ins = nc.vector.tensor_tensor(
                        dst, ps[:, half, b, :].rearrange("p (j c) -> p j c", j=CH),
                        rstd[:, :].rearrange("p (j c) -> p j c", j=CH), mult)
                ins.then_inc(free[half], 1)

            def split_g(k):
                wait_emptied(dve, f"y{k // 2}")
                dve.wait_ge(w_used, 24 + k // 2 + 1)
                split_tile(UG[:, k, :, :].rearrange("p j c -> p (j c)"), H_hi[:, k, :], H_lo[:, k, :],
                           g_rdy)

            def split_pooled(k):
                split_tile(V[:, k, :, :].rearrange("p j c -> p (j c)"), H_hi[:, 8 + k, :],
                           H_lo[:, 8 + k, :], pool_rdy)

            build_q(0)
            projection(0)
            def square_phase():
                tt(v_[0], v_[14], v_[14], mult)
                tt(v_[1], v_[12], v_[12], mult)
                tt(v_[2], v_[14], v_[12], mult)
                settle()
                tt(v_[14], v_[0], v_[1], sub)
                ts(v_[12], v_[2], 2.0, None, mult)
                settle()

            for _ in range(3):
                tt(v_[10], v_[10], v_[10], mult)
                square_phase()
            step(nc.vector.memset(ph_c[:, :, 0:1], 1.0))
            step(nc.vector.memset(ph_s[:, :, 0:1], 0.0))
            settle()
            n = 1
            while n < NC:
                cmul((ph_c[:, :, n:2 * n], ph_s[:, :, n:2 * n]), (ph_c[:, :, 0:n], ph_s[:, :, 0:n]),
                     (cols(v_[14], n), cols(v_[12], n)), pt[0][:, :, 0:n], pt[1][:, :, 0:n])
                n *= 2
                if n < NC:
                    square_phase()
            nc.vector.memset(s_re[:, :, 0:1], 0.0).then_inc(s_cleared, 1)
            nc.vector.memset(s_im[:, :, 0:1], 0.0).then_inc(s_cleared, 1)

            for pair in range(9, P_GLU):
                if pair % 8 == 7:
                    if pair == P_GLU - 1:
                        for k in range(4, 6):
                            split_g(k)
                    projection(pair // 8)
                for kind, r in after.get(pair, []):
                    small(kind, r)

            wait_emptied(dve, "in3")
            dve.wait_ge(consts, 6 + 2 * CH)
            for k in range(4):
                for level in range(levels(k)):
                    shifted_add(nc.vector, step, settle, dpl, k, level)
                step(window_mean(nc.vector, step, settle, dpl, dpl_s, k))
                settle()
                split_pooled(k)
            for k in range(6, 8):
                split_g(k)
            def gated(s):
                wait_emptied(dve, f"gl{s}")
                for b in range(4):
                    tt(gsig[:, b, :], gsig[:, b, :],
                       UG[:, 4 * s + b, :, :].rearrange("p j c -> p (j c)"), mult)
                settle()

            def split_gated(s):
                for b in range(4):
                    split_tile(gsig[:, b, :], M_hi[:, 4 * s + b, :], M_lo[:, 4 * s + b, :], ms_rdy)

            def pool_mixed(s):
                dve.wait_ge(w_used, P_POOL + s + 1)
                half = jobs[f"po{s}"][0]
                for b in range(4):
                    k = 4 * s + b
                    ins = nc.vector.tensor_scalar(pmix[:, b, :], ps[:, half, b, :], vecs[:, 40 + k:41 + k],
                                                  vecs[:, 48 + k:49 + k], add, mult)
                ins.then_inc(free[half], 1)
                wait_emptied(dve, f"po{s}")

            def split_pool_mixed(s):
                for b in range(4):
                    split_tile(pmix[:, b, :], H_hi[:, 4 * s + b, :], H_lo[:, 4 * s + b, :], mp_rdy)

            gated(0)
            split_gated(0)
            for k in range(4, 8):
                dve.wait_ge(pooled, k - 3)
                split_pooled(k)
            gated(1)
            pool_mixed(0)
            split_gated(1)
            split_pool_mixed(0)
            dve.wait_ge(mp_rdy, 4)
            pool_mixed(1)
            split_pool_mixed(1)
            dve.wait_ge(mp_rdy, 8)

            def ffn_input(k):
                g = vecs[:, 16 + k:17 + k]
                ts(H_hi[:, (k + 8) % 16, :], resT[:, k, :], g, None, mult)
                settle()
                nc.vector.scalar_tensor_tensor(out=H_lo[:, (k + 8) % 16, :], in0=resT[:, k, :], scalar=g,
                                               in1=H_hi[:, (k + 8) % 16, :].bitcast(f32),
                                               op0=mult, op1=sub).then_inc(h_rdy, 1)

            def add_square(k):
                tt(sqa[:, :] if k == 0 else sqt[:, :], resT[:, k, :], resT[:, k, :], mult)
                settle()
                if k:
                    ins = nc.vector.tensor_tensor(sqa[:, :], sqa[:, :], sqt[:, :], add)
                    if k < KT - 1:
                        step(ins)
                        settle()
                    else:
                        ins.then_inc(acc_rdy, 1)

            for s in range(4):
                wait_aux(dve, f"wo{s}")
                half = jobs[f"wo{s}"][0]
                for b in range(4):
                    ins = nc.vector.tensor_copy(resT[:, 4 * s + b, :], ps[:, half, b, :])
                ins.then_inc(free[half], 1)
                wait_emptied(dve, f"wo{s}")
                if s < 2:
                    for b in range(4):
                        ffn_input(4 * s + b)
                if s == 3:
                    for k in range(8, 16):
                        ffn_input(k)
                for b in range(4):
                    add_square(4 * s + b)
            wait_aux(dve, "rms2")
            half = jobs["rms2"][0]
            nc.vector.tensor_copy(sqt[:, :], ps[:, half, 0, :]).then_inc(free[half], 1)
            wait_emptied(dve, "rms2")
            nc.vector.tensor_scalar(sqa[:, :], sqt[:, :], 1.0 / D_MODEL, EPS, mult, add) \
                .then_inc(var_rdy, 1)
            inverse_root(rstd[:, :], sqa[:, :], sqt[:, :], 2)

            def gate_out(half, used):
                dve.wait_ge(w_used, used)
                for b in range(4):
                    ins = nc.vector.tensor_tensor(gate[:, b, :], ps[:, half, b, :], rstd[:, :], mult)
                ins.then_inc(free[half], 1)

            def gate_scale(first):
                for b in range(4):
                    dve.wait_ge(silu_done, first + b)
                    nc.vector.tensor_tensor(gate[:, b, :], gate[:, b, :], rstd[:, :], mult) \
                        .then_inc(scaled_rdy, 1)

            def up_out(half, used, scaled, freed, ff, new):
                dve.wait_ge(w_used, used)
                dve.wait_ge(scaled_rdy, scaled)
                for b0 in (0, 2):
                    for b in (b0, b0 + 1):
                        ins = nc.vector.tensor_tensor(gate[:, b, :], ps[:, half, b, :], gate[:, b, :],
                                                      mult)
                    if b0 == 0:
                        ins.then_inc(ff_new, 1)
                        dve.wait_ge(ff_new, new)
                    else:
                        ins.then_inc(free[half], 1)
                        dve.wait_ge(*freed)
                    for b in (b0, b0 + 1):
                        nc.vector.tensor_copy(F_hi[:, b, :], gate[:, b, :]).then_inc(ff_hi, 1)
                    for b in (b0, b0 + 1):
                        dve.wait_ge(ff_hi, ff + b)
                        nc.vector.tensor_tensor(F_lo[:, b, :], gate[:, b, :],
                                                F_hi[:, b, :].bitcast(f32), sub).then_inc(ff_rdy, 1)

            gate_out(jobs["gate"][0], P_UP)
            gate_scale(1)
            half, _, then = jobs["up"]
            up_out(half, P_LOOP, 4, (free[half], then), 1, 1)
            wait_emptied(dve, "tok3")
            with nc.vector.Fori(0, FG - 1) as i:
                dve.wait_ge(ff_rdy, i * 4 + 4)
                gate_out(LOOP["gate"][0], i * PER + (P_LOOP + 8))
                for c in range(4):
                    half = LOOP[f"down{c}"][0]
                    dve.wait_ge(w_used, i * PER + (P_LOOP + 8 + 2 * c + 2))
                    for t in range(4):
                        cell = res_tok[:, t, NW * c:NW * c + NW]
                        ins = nc.vector.tensor_tensor(cell, ps[:, half, t, :], cell, add)
                    ins.then_inc(free[half], 1)
                    if c == 2:
                        gate_scale(i * 4 + 5)
                up_out(LOOP["up"][0], i * PER + (P_LOOP + PER), i * 4 + 8, loop_free("up", i, 1),
                       i * 4 + 5, i + 2)
            dve.wait_ge(gf_loaded, 16)
            for t in range(4):
                for c in range(4):
                    dve.wait_ge(down_done, 4 * t + c + 1)
                    cell = res_tok[:, t, NW * c:NW * c + NW]
                    nc.vector.tensor_tensor(cell, ps[:, LAST_HALF[t], c, :], cell, add).then_inc(fin_rdy, 1)
                dve.wait_ge(fin_sq, 4 * t + 4)
                ts_ = slice(t, t + 1)
                step(nc.vector.tensor_reduce(rtok[:, ts_], ssq[:, t, :], AX.X, add))
                settle()
                nc.vector.tensor_scalar(vtok[:, ts_], rtok[:, ts_], 1.0 / D_MODEL, EPS, mult, add) \
                    .then_inc(var_rdy, 1)
                inverse_root(rtok[:, ts_], vtok[:, ts_], stok[:, ts_], 3 + t)
                for part in range(2):
                    cs = slice(2 * NW * part, 2 * NW * (part + 1))
                    nc.vector.scalar_tensor_tensor(out=res_tok[:, t, cs], in0=res_tok[:, t, cs],
                                                   scalar=rtok[:, ts_], in1=gfin[:, cs],
                                                   op0=mult, op1=mult).then_inc(o_rdy, 1)

        @block.tensor
        def _(pe):
            mm = nc.tensor.matmul

            def three(o, a, b, first, last):
                (ah, al), (bh, bl) = a, b
                for part, (a_, b_) in enumerate(((ah, bh), (ah, bl), (al, bh))):
                    ins = mm(o, a_, b_, start=first and part == 0, stop=last and part == 2)
                return ins

            def weight_pair(n, half, acts, first, last):
                wh, wl = split_slot(n)
                for kt in range(2):
                    for b in range(4):
                        cs = slice(P * b, P * b + P)
                        ins = three(ps[:, half, b, :], (wh[:, kt, cs], wl[:, kt, cs]), acts[kt],
                                    first and kt == 0, last and kt == 1)
                return ins

            def h_at(k):
                return H_hi[:, k, :], H_lo[:, k, :]

            def m_at(k):
                return M_hi[:, k, :], M_lo[:, k, :]

            pe.wait_ge(consts, 6)
            pe.wait_ge(gains_loaded, 16)
            half = wait_half(pe, "gains")
            nc.tensor.transpose(ps[:, half, 0, 0:KT], gain_rows[:, :], ident[0:KT, 0:KT]) \
                .then_inc(aux_done, 1)

            def small(kind, r):
                half = wait_half(pe, key(kind, r))
                if kind == "xt":
                    pe.wait_ge(x_loaded[r], 32)
                    for b in range(4):
                        for t in range(4):
                            k = 4 * r + b
                            ins = nc.tensor.transpose(ps[:, half, b, P * t:P * t + P],
                                                      x_tok[:, t, P * k:P * k + P], ident[:, :])
                elif kind == "vec":
                    pe.wait_ge(rows_loaded, 16 * 14)
                    ins = nc.tensor.transpose(ps[:, half, 0, 0:P], vec_rows[:, :], ident[:, :])
                elif kind == "ct":
                    pe.wait_ge(c_loaded, 32)
                    for k in range(2):
                        for b in range(4):
                            ins = nc.tensor.transpose(
                                ps[:, half, k, P * b:P * b + P],
                                c_raw[k][:, 2 * b:2 * b + 2, :].rearrange("p b s -> p (b s)"), ident[:, :])
                elif kind == "rms":
                    pe.wait_ge(diag_rdy, 4)
                    ins = mm(ps[:, half, 0, :], ones[:, :], diag[:, :, :].rearrange("p t n -> p (t n)"),
                             start=True, stop=True)
                elif kind == "tok":
                    for k in range(KT):
                        ins = nc.tensor.transpose(ps[:, half, k // 4, P * (k % 4):P * (k % 4) + P],
                                                  resT[:, k, P * r:P * r + P], ident[:, :])
                elif kind == "rms2":
                    pe.wait_ge(acc_rdy, 1)
                    ins = mm(ps[:, half, 0, :], ones[:, :], sqa[:, :], start=True, stop=True)
                elif kind == "a":
                    pe.wait_ge(q_rdy, r + 1)
                    for k in range(2):
                        for g in range(8):
                            ins = nc.tensor.transpose(
                                ps[:, half, 2 * k + g // 4, P * (g % 4):P * (g % 4) + P],
                                QR[k][:, g, :, :].rearrange("p d h -> p (d h)"), ident[:, :])
                elif kind == "b":
                    pe.wait_ge(q2_rdy, 2 * (r + 1))
                    for q in range(2):
                        rows = slice(64 * q, 64 * q + 64)
                        for d in range(CH):
                            o = ps[:, half, 2 * q + d // 4, P * (d % 4):P * (d % 4) + P]
                            mm(o, Q2[0][rows, d, :, :].rearrange("p g h -> p (g h)"), ct_re[rows, r, :, :].rearrange("p g h -> p (g h)"),
                               start=True, stop=False)
                            ins = mm(o, Q2[1][rows, d, :, :].rearrange("p g h -> p (g h)"),
                                     ct_in[rows, r, :, :].rearrange("p g h -> p (g h)"),
                                     start=False, stop=True)
                elif kind == "e":
                    wait_emptied(pe, f"a{r}")
                    pe.wait_ge(u8_loaded, 16 * CH * (r + 1))
                    for k in range(2):
                        for q in range(2):
                            rows = slice(64 * q, 64 * q + 64)
                            for g in range(8):
                                ins = mm(ps[rows, half, k, NC * g:NC * g + NC], QT[:, k, g, rows],
                                         U8[:, q, g, :], start=True, stop=True)
                elif kind == "i":
                    pe.wait_ge(s_rdy, r + 1)
                    pe.wait_ge(r_rdy, r + 1)
                    for q in range(2):
                        rows = slice(64 * q, 64 * q + 64)
                        for g in range(8):
                            o = ps[0:64, half, 2 * q + g // 4, P * (g % 4):P * (g % 4) + P]
                            for k, st in enumerate((s_re, s_im)):
                                ins = mm(o, st[rows, g, 0:NC],
                                         QR[k][rows, g, :, :].rearrange("p j h -> p (j h)"),
                                         start=k == 0, stop=k == 1)
                elif kind == "y":
                    wait_emptied(pe, f"i{r}")
                    pe.wait_ge(bd_rdy, 2 * (r + 1))
                    for q in range(2):
                        o = ps[:, half, q, :]
                        for d in range(CH):
                            mm(o[:, NC * d:], BD[:, q, d, :],
                               UG[:, 2 * r + q, 0:CH - d, :].rearrange("p j c -> p (j c)"),
                               start=d == 0, stop=False)
                        for j in range(CH):
                            ins = mm(o[:, NC * j:NC * j + NC], yt[:, j, q, :], ident[0:64, 0:NC],
                                     start=False, stop=j == CH - 1)
                ins.then_inc(aux_done, 1)

            small("xt", 0)
            for n in range(P_GLU):
                s, m = divmod(n, 8)
                half = jobs[f"in{s}"][0]
                if m == 0:
                    wait_half(pe, f"in{s}")
                if s == 0 and m % 2 == 0:
                    pe.wait_ge(x_lo, m // 2 + 1)
                elif s == 0:
                    wait_emptied(pe, f"xt{m // 2}")
                pe.wait_ge(lo_done, n + 1)
                weight_pair(n, half, (h_at(2 * m), h_at(2 * m + 1)), m == 0, m == 7).then_inc(w_used, 1)
                for kind, r in after.get(n, []):
                    small(kind, r)
            for n in range(P_GLU, P_POOL):
                s, m = divmod(n - P_GLU, 4)
                half = jobs[f"gl{s}"][0]
                if m == 0:
                    wait_half(pe, f"gl{s}")
                if s == 0:
                    pe.wait_ge(g_rdy, 2 * m + 2)
                pe.wait_ge(lo_done, n + 1)
                weight_pair(n, half, (h_at(2 * m), h_at(2 * m + 1)), m == 0, m == 3).then_inc(w_used, 1)
                for kind, r in after.get(n, []):
                    small(kind, r)
            for s in range(2):
                n = P_POOL + s
                half = wait_half(pe, f"po{s}")
                pe.wait_ge(pool_rdy, 4 * s + 4)
                pe.wait_ge(lo_done, n + 1)
                wh, wl = split_slot(n)
                for b in range(4):
                    g, mt = divmod(b, 2)
                    for kt in range(2):
                        cs = slice(256 * kt + P * mt, 256 * kt + P * mt + P)
                        ins = three(ps[:, half, b, :], (wh[:, g, cs], wl[:, g, cs]),
                                    h_at(8 + 4 * s + 2 * g + kt), kt == 0, kt == 1)
                ins.then_inc(w_used, 1)
            for n in range(P_OUT, P_GATE):
                s, m = divmod(n - P_OUT, 8)
                half = jobs[f"wo{s}"][0]
                if m == 0:
                    wait_half(pe, f"wo{s}")
                if s == 0:
                    pe.wait_ge(*((ms_rdy, 2 * m + 2) if m < 4 else (mp_rdy, 2 * (m - 4) + 2)))
                pe.wait_ge(lo_done, n + 1)
                at_k = m_at if m < 4 else h_at
                weight_pair(n, half, (at_k(2 * (m % 4)), at_k(2 * (m % 4) + 1)), m == 0, False) \
                    .then_inc(w_used, 1)
                if m == 7:
                    pe.wait_ge(x_loaded[s], 64)
                    for b in range(4):
                        for t in range(4):
                            ins = mm(ps[:, half, b, P * t:P * t + P],
                                     x_tok[:, t, P * (4 * s + b):P * (4 * s + b) + P], ident[:, :],
                                     start=False, stop=t == 3)
                    ins.then_inc(aux_done, 1)

            def ffn_pair(n, half, m, lo=None):
                pe.wait_ge(lo_done, n + 1 if lo is None else lo)
                acts = [h_at((k + 8) % 16) for k in (2 * m, 2 * m + 1)]
                weight_pair(n, half, acts, m == 0, m == 7).then_inc(w_used, 1)

            def down_pair(n, half, kp, lo=None):
                pe.wait_ge(lo_done, n + 1 if lo is None else lo)
                wh, wl = split_slot(n)
                for kt in range(2):
                    for t in range(4):
                        ts_ = slice(P * t, P * t + P)
                        k = 2 * kp + kt
                        ins = three(ps[:, half, t, :], (F_hi[:, k, ts_], F_lo[:, k, ts_]),
                                    (wh[:, kt, :], wl[:, kt, :]), k == 0, k == 3)
                ins.then_inc(w_used, 1)

            half = wait_half(pe, "gate")
            for m in range(8):
                pe.wait_ge(h_rdy, 2 * m + 2)
                ffn_pair(P_GATE + m, half, m)
                for kind, r in after.get(P_GATE + m, []):
                    small(kind, r)
            half = wait_half(pe, "up")
            for m in range(8):
                ffn_pair(P_UP + m, half, m)
            with nc.tensor.Fori(0, FG - 1) as i:
                def lo(m):
                    return i * PER + (P_LOOP + m + 1)
                pe.wait_ge(*loop_free("gate", i, 0))
                for m in range(8):
                    ffn_pair(P_LOOP + m, LOOP["gate"][0], m, lo(m))
                pe.wait_ge(ff_rdy, i * 4 + 4)
                for c in range(4):
                    pe.wait_ge(*loop_free(f"down{c}", i, 0))
                    for kp in range(2):
                        down_pair(P_LOOP + 8 + 2 * c + kp, LOOP[f"down{c}"][0], kp, lo(8 + 2 * c + kp))
                pe.wait_ge(*loop_free("up", i, 0))
                for m in range(8):
                    ffn_pair(P_LOOP + 16 + m, LOOP["up"][0], m, lo(16 + m))
            for t in range(4):
                half, ts_ = LAST_HALF[t], slice(P * t, P * t + P)
                if t < 2:
                    pe.wait_ge(free[half], loop_uses[half] + 3 * (FG - 1))
                for c in range(4):
                    if t >= 2:
                        pe.wait_ge(fin_rdy, 4 * (t - 2) + c + 1)
                    for k in range(4):
                        if c == t == 0 and k % 2 == 0:
                            pe.wait_ge(ff_rdy, 4 * (FG - 1) + k + 2)
                        kp, kt = divmod(k, 2)
                        n = P_LAST + 2 * c + kp
                        if t == 0 and kt == 0:
                            pe.wait_ge(lo_done, n + 1)
                        wh, wl = split_slot(n)
                        ins = three(ps[:, half, c, :], (F_hi[:, k, ts_], F_lo[:, k, ts_]),
                                    (wh[:, kt, :], wl[:, kt, :]), k == 0, k == 3)
                    ins.then_inc(down_done, 1)


_INS = ["x", "norm_mix", "w_in", "lambda_re", "lambda_im", "log_step", "b_re", "b_im", "c_re", "c_im",
        "d_skip", "w_glu", "b_glu", "w_pool", "b_pool", "pool_scale", "w_out", "norm_ffn", "w_gate",
        "w_up", "w_down", "norm_final"]


def kernel(**inputs):
    import numpy as np
    import concourse.bacc as bacc
    from concourse import mybir as mb
    from concourse.bass_utils import run_bass_kernel_spmd

    nc = bacc.Bacc("TRN2", target_bir_lowering=False, num_devices=1)
    arrays, args = {}, []
    for name in _INS:
        a = np.ascontiguousarray(inputs[name])
        arrays[f"in_{name}"] = a
        args.append(nc.dram_tensor(f"in_{name}", a.shape, mb.dt.from_np(a.dtype), kind="ExternalInput").ap())
    args.append(nc.dram_tensor("out_0", (1, SEQ, D_MODEL), mb.dt.float32, kind="ExternalOutput").ap())
    emit(nc, *args)
    r = run_bass_kernel_spmd(nc, [arrays], core_ids=[0])
    return r.results[0]["out_0"]
```

```python
import math
from contextlib import ExitStack

import concourse.bass as bass
from concourse import mybir

D_MODEL = 2048
SEQ = 512
STATE, GCH = 64, 16
WINDOWS = (2, 4, 8, 16)
D_FF = ((8 * D_MODEL // 3 + 255) // 256) * 256
EPS = 1e-6

P = 128
KT = D_MODEL // P
NW = 512
CH = 8
NC = SEQ // CH
ROUNDS = 4
FG = D_FF // NW

RAW_SLOTS = 3
SPLIT_SLOTS = 3
WARM = 16
LATE_SLOTS = 8 - SPLIT_SLOTS


def emit(nc, x, norm_mix, w_in, lambda_re, lambda_im, log_step, b_re, b_im, c_re, c_im, d_skip,
         w_glu, b_glu, w_pool, b_pool, pool_scale, w_out, norm_ffn, w_gate, w_up, w_down,
         norm_final, out):
    f32, f32r, i32 = mybir.dt.float32, mybir.dt.float32r, mybir.dt.int32
    ALU, ACT, AX = mybir.AluOpType, mybir.ActivationFunctionType, mybir.AxisListType
    mult, add, sub = ALU.mult, ALU.add, ALU.subtract

    base = (nc.sbuf_base + 63) // 64 * 64
    end = nc.sbuf_usable_end

    def at(name, shape, dt, offset):
        size = 4
        for n in shape[1:]:
            size *= n
        assert offset + size <= end, (name, offset, size, end)
        return nc.alloc_sbuf_tensor_at(name, shape, dt, offset=offset)

    KB = 1024
    R_H = base
    R_A = R_H + 64 * KB
    R_W = R_A + 32 * KB
    R_S = R_W + RAW_SLOTS * 4 * KB + SPLIT_SLOTS * 8 * KB

    H_hi = at("H_hi", [P, KT, SEQ], f32r, R_H)
    H_lo = at("H_lo", [P, KT, SEQ], f32r, R_H + 32 * KB)
    x_tok = at("x_tok", [P, 4, D_MODEL], f32, R_A)
    UG = at("UG", [P, 8, CH, NC], f32, R_A)
    V = at("V", [P, 8, CH, NC], f32, R_A + 16 * KB)
    res_tok = at("res_tok", [P, 4, D_MODEL], f32, R_A)
    raw = [at(f"raw{i}", [P, 2, NW], f32, R_W + 4 * KB * i) for i in range(RAW_SLOTS)]
    R_W2 = R_W + RAW_SLOTS * 4 * KB
    w_hi = [at(f"w_hi{i}", [P, 2, NW], f32r, R_W2 + 8 * KB * i) for i in range(SPLIT_SLOTS)]
    w_lo = [at(f"w_lo{i}", [P, 2, NW], f32r, R_W2 + 8 * KB * i + 4 * KB) for i in range(SPLIT_SLOTS)]

    top = [R_S]

    def take(name, shape, dt=f32, part=P):
        size = 4
        for n in shape:
            size *= n
        t = at(name, [part, *shape], dt, top[0])
        top[0] += (size + 31) // 32 * 32
        return t

    ident = take("ident", [P])
    ones = take("ones", [P])
    vecs = take("vecs", [P])
    rstd = take("rstd", [SEQ])
    ssq = take("ssq", [4, 4])
    rtok = take("rtok", [4])
    vtok = take("vtok", [4])
    stok = take("stok", [4])
    inv_n = take("inv_n", [2, CH])
    R_T = top[0]
    mask = take("mask", [8, GCH])
    bb_re = take("bb_re", [4, 8, GCH])
    bb_im = take("bb_im", [4, 8, GCH])
    ct_re = take("ct_re", [4, 8, GCH])
    ct_in = take("ct_in", [4, 8, GCH])
    lp_re = take("lp_re", [CH + 1, 32])
    lp_im = take("lp_im", [CH + 1, 32])
    par = take("par", [22, 32])
    pari = take("pari", [32], i32)
    ph_c = take("ph_c", [32, NC])
    ph_s = take("ph_s", [32, NC])
    R_Q = top[0]
    QR = [take(f"q{k}", [8, CH, GCH]) for k in ("re", "im")]
    zr = take("zr", [8, NC])
    zi = take("zi", [8, NC])
    zt = take("zt", [8, NC])
    BD = take("BD", [2, CH, P])
    Q2 = [at(f"q2{k}", [P, CH, 8, GCH], f32, top[0] - 8 * KB + 4 * KB * n)
          for n, k in enumerate(("re", "im"))]
    R_QT = top[0]
    QT = take("QT", [2, 8, P])
    U8 = take("U8", [2, 8, NC])
    s_re = take("s_re", [8, NC + 1])
    s_im = take("s_im", [8, NC + 1])
    yt = at("yt", [P, CH // 2, 2, P], f32, R_QT)
    tmp1024 = at("tmp1024", [P, 8, CH, GCH], f32, R_Q + 8 * KB)
    c_raw = [at(f"c_raw{k}", [P, 8, STATE], f32, R_Q + 2 * KB * k) for k in range(2)]
    b_raw = [at(f"b_raw{k}", [P, 4, 8, GCH], f32, R_QT + 2 * KB * k) for k in range(2)]
    t512 = [at(f"t512_{k}", [P, 32, GCH], f32, R_Q + 4 * KB + 2 * KB * k) for k in range(2)]
    pw = [at(f"pw{k}", [P, 4, 32], f32, R_Q + 4 * KB + 512 * k) for k in range(2)]
    pt = [at(f"pt{k}", [P, 32, 32], f32, R_A + 16 * KB + 4 * KB * k) for k in range(2)]
    vec_rows = at("vec_rows", [P, P], f32, R_QT + 4 * KB)
    gain_rows = at("gain_rows", [KT, P], f32, R_QT + 6 * KB)
    lstep = at("lstep", [P, 4, 8], f32, R_QT + 5 * KB)
    sq_junk = at("sq_junk", [P, D_MODEL], f32, R_Q + 14 * KB)
    diag = at("diag", [P, 4, P], f32, R_Q + 8 * KB)

    M_hi = at("M_hi", [P, 8, SEQ], f32r, R_T)
    M_lo = at("M_lo", [P, 8, SEQ], f32r, R_T + 16 * KB)
    gsig = at("gsig", [P, 4, SEQ], f32, R_T + 32 * KB)
    pmix = at("pmix", [P, 4, SEQ], f32, R_T + 40 * KB)
    pl = [take(f"pl{k}", [CH, NC]) for k in range(2)]
    pl_s = take("pl_s", [2, CH])
    dpl = [at(f"dpl{k}", [P, CH, NC], f32, R_Q + 8 * KB + 2 * KB * k) for k in range(2)]
    dpl_s = at("dpl_s", [P, 2, CH], f32, R_Q + 12 * KB)
    F_hi = at("F_hi", [P, 4, SEQ], f32r, R_T)
    F_lo = at("F_lo", [P, 4, SEQ], f32r, R_T + 8 * KB)
    gate = at("gate", [P, 4, SEQ], f32, R_T + 16 * KB)
    fsq = at("fsq", [P, NW], f32, R_H)
    gfin = at("gfin", [P, D_MODEL], f32, R_T + 24 * KB)
    late = [[at(f"late_{part}{m}", [P, 2, NW], f32r, R_T + (32 + 8 * m + 4 * k) * KB)
             for k, part in enumerate(("hi", "lo"))] for m in range(LATE_SLOTS)]
    u_dram = nc.dram_tensor("u_dram", (8, P, CH, NC), f32).ap()

    ctx = ExitStack()
    with ctx:
        ps = ctx.enter_context(nc.psum_tensor("ps", [P, 2, 4, 512], f32))

        def sem(name):
            return ctx.enter_context(nc.semaphore(name))

        free = [sem("half0_free"), sem("half1_free")]
        x_loaded = [sem(f"x_loaded{i}") for i in range(4)]
        raw_full = [sem(f"raw_full{i}") for i in range(RAW_SLOTS)]
        hi_done = sem("w_hi_done")
        lo_done = sem("w_lo_done")
        w_used = sem("w_used")
        aux_done = sem("aux_done")
        gains_loaded = sem("gains_loaded")
        rows_loaded = sem("vector_rows_loaded")
        step_loaded = sem("log_step_loaded")
        b_loaded = sem("b_loaded")
        c_loaded = sem("c_loaded")
        u_stored = sem("u_stored")
        u8_loaded = sem("u8_loaded")
        gf_loaded = sem("final_gain_loaded")
        out_stored = sem("out_stored")
        consts = sem("consts_ready")
        h_hi = sem("h_hi")
        h_lo = sem("h_lo")
        row_sq = sem("row_squares")
        trig_in = sem("trig_in")
        trig = sem("trig")
        chain = sem("dve_chain")
        gp_chain = sem("gp_chain")
        var_rdy = sem("mean_square_ready")
        root_done = sem("root_done")
        diag_rdy = sem("diag_ready")
        q_rdy = sem("q_ready")
        q2_rdy = sem("q2_ready")
        r_rdy = sem("r_ready")
        bd_rdy = sem("bd_ready")
        s_cleared = sem("s_cleared")
        s_rdy = sem("s_ready")
        pooled = sem("pooled")
        pool_rdy = sem("pooled_split")
        g_rdy = sem("g_split")
        ms_rdy = sem("mixed_ssm_split")
        mp_rdy = sem("mixed_pool_split")
        silu_done = sem("silu_done")
        scaled_rdy = sem("silu_scaled")
        up_half = sem("up_half_done")
        ff_new = sem("ff_products")
        ff_hi = sem("ff_hi")
        ff_rdy = sem("ff_split")
        down_done = sem("last_down_done")
        fin_rdy = sem("final_tiles")
        fin_sq = sem("final_squares")
        o_rdy = sem("out_rows")

        jobs = {}
        uses = [0, 0]

        def job(name, half):
            jobs[name] = (half, uses[half], uses[half] + 1)
            uses[half] += 1

        P_GLU, P_POOL, P_OUT, P_GATE, P_UP, P_LOOP = 32, 40, 42, 74, 82, 90
        PER = 24
        P_LAST = P_LOOP + PER * (FG - 1)
        assert PER % RAW_SLOTS == 0 and PER % SPLIT_SLOTS == 0
        IN_COLS = (0, 1, 3, 2)
        after = {0: [("xt", 1)], 1: [("vec", 0)], 2: [("xt", 2)], 3: [("xt", 3)], 4: [("ct", 0)],
                 5: [("rms", 0)]}
        for r in range(ROUNDS):
            for kind, d in (("a", 0), ("b", 1), ("e", 2), ("i", 5), ("y", 6)):
                after.setdefault(9 + 6 * r + d, []).append((kind, r))
        for p in after:
            after[p].sort(key=lambda job_: job_[0] == "a")
        for s, p in enumerate((P_OUT + 8, P_OUT + 16, P_OUT + 28, P_GATE)):
            after[p] = [("rt", s)]
        after[P_GATE + 6] = [("rms2", 0)]

        def out_pair(n):
            s, m = divmod(n - P_OUT, 8)
            return s, m, m if s < 3 else (m + 4) % 8

        def key(kind, r):
            return f"{kind}{r}" if kind in ("xt", "rt") or kind in "abeiy" else kind

        job("gains", 0)
        job("xt0", 0)
        aux_order = ["gains", "xt0"]
        products = ([("in", s, 8) for s in range(4)] + [("gl", s, 4) for s in range(2)]
                    + [("po", s, 1) for s in range(2)] + [("wo", s, 8) for s in range(4)]
                    + [("gate", None, 8), ("up", None, 8)])
        n = 0
        for number, (name, s, pairs) in enumerate(products):
            half = (number + 1) % 2
            job(name if s is None else f"{name}{s}", half)
            for p in range(n, n + pairs):
                for kind, r in after.get(p, []):
                    job(key(kind, r), 1 - half)
                    aux_order.append(key(kind, r))
            n += pairs
        aux_count = {name: n + 1 for n, name in enumerate(aux_order)}
        loop_uses = tuple(uses)
        G = jobs["gate"][0]
        LOOP = {"gate": (G, 0), "down0": (1 - G, 0), "down1": (G, 1), "down2": (1 - G, 1),
                "down3": (G, 2), "up": (1 - G, 2)}
        assert jobs["up"][0] == 1 - G
        LAST_HALF = (G, 1 - G, G, 1 - G)

        def split_slot(n):
            m = n - P_LAST
            if 0 <= m < LATE_SLOTS:
                return late[m]
            slot = (m - LATE_SLOTS if m >= 0 else n) % SPLIT_SLOTS
            return w_hi[slot], w_lo[slot]

        def late_place(c, kp):
            return 4 * kp + c

        def slot_used(n):
            m = n - P_LAST
            if n < SPLIT_SLOTS or 0 <= m < LATE_SLOTS:
                return None
            return n - SPLIT_SLOTS + 1 - (LATE_SLOTS if m >= 0 else 0)

        def h_tile(kind, s, b):
            k = 4 * s + b
            return (k, k) if kind == "xt" else (KT + k, (k + 8) % KT)

        def wait_half(eng, name):
            half, need, _ = jobs[name]
            if need:
                eng.wait_ge(free[half], need)
            return half

        def wait_emptied(eng, name):
            half, _, then = jobs[name]
            eng.wait_ge(free[half], then)

        def wait_aux(eng, name):
            eng.wait_ge(aux_done, aux_count[name])

        def loop_free(name, i, after):
            half, nth = LOOP[name]
            return free[half], i * 3 + (loop_uses[half] + nth + after)

        def pair_src(w, rows, cols):
            return w[0, rows:rows + 2 * P, cols].rearrange("(k p) n -> p k n", p=P)

        def static_src(n):
            def cols(s):
                return slice(s * NW, (s + 1) * NW)
            if n < P_GLU:
                return pair_src(w_in, 256 * (n % 8), cols(IN_COLS[n // 8]))
            if n < P_POOL:
                s, m = divmod(n - P_GLU, 4)
                return pair_src(w_glu, 256 * m, cols(s))
            if n < P_OUT:
                m = n - P_POOL
                return w_pool[0, 2 * m:2 * m + 2, :, :].rearrange("g (k p) d -> p g k d", p=P)
            if n < P_GATE:
                s, _, m = out_pair(n)
                return pair_src(w_out, 256 * m, cols(s))
            if n < P_UP:
                return pair_src(w_gate, 256 * (n - P_GATE), cols(0))
            return pair_src(w_up, 256 * (n - P_UP), cols(0))

        def levels(k):
            return WINDOWS[k // 2].bit_length() - 1

        def level_sums(sums, k, level):
            return V[:, k, :, :] if level == 0 else sums[level % 2][:, :, :]

        def shifted_add(engine, step, settle, sums, k, level):
            s, a, o = 2 ** level, level_sums(sums, k, level), level_sums(sums, k, level + 1)
            if s < CH:
                step(engine.tensor_tensor(o[:, s:, :], a[:, s:, :], a[:, :CH - s, :], add))
                step(engine.tensor_tensor(o[:, 0:s, 1:], a[:, 0:s, 1:], a[:, CH - s:, :NC - 1], add))
                step(engine.tensor_copy(o[:, 0:s, 0:1], a[:, 0:s, 0:1]))
            else:
                step(engine.tensor_tensor(o[:, :, 1:], a[:, :, 1:], a[:, :, :NC - 1], add))
                step(engine.tensor_copy(o[:, :, 0:1], a[:, :, 0:1]))
            settle()

        def window_mean(engine, step, settle, sums, head, k):
            w, v, cur = WINDOWS[k // 2], V[:, k, :, :], level_sums(sums, k, levels(k))
            nj, ncol = min(w, CH), max(1, w // CH)
            for c in range(ncol):
                step(engine.tensor_tensor(head[:, c, 0:nj], cur[:, 0:nj, c], inv_n[:, c, 0:nj], mult))
            settle()
            for c in range(ncol):
                step(engine.tensor_tensor(head[:, c, 0:nj], head[:, c, 0:nj], v[:, 0:nj, c], sub))
            if engine is nc.vector:
                settle()
                step(engine.scalar_tensor_tensor(out=v, in0=cur, scalar=1.0 / w, in1=v,
                                                 op0=mult, op1=sub))
            else:
                step(engine.tensor_scalar(cur, cur, 1.0 / w, None, mult))
                settle()
                step(engine.tensor_tensor(v, cur, v, sub))
            settle()
            for c in range(ncol):
                ins = engine.tensor_copy(v[:, 0:nj, c], head[:, c, 0:nj])
                if c < ncol - 1:
                    step(ins)
            return ins

        block = ctx.enter_context(nc.Block())

        @block.sync
        def _(sp):
            def load(n, src, done=None):
                if n >= RAW_SLOTS:
                    sp.wait_ge(lo_done, n - RAW_SLOTS + 1 if done is None else done)
                dst = raw[n % RAW_SLOTS][:, :, :]
                if P_POOL <= n < P_OUT:
                    dst = dst.rearrange("p g (k d) -> p g k d", k=2)
                sp.dma_start(dst, src).then_inc(raw_full[n % RAW_SLOTS], 16)

            def load_x(s):
                for j in range(2):
                    sp.dma_start(x_tok[64 * j:64 * j + 64, :, NW * s:NW * s + NW],
                                 x[0].rearrange("(c t j) n -> j c t n", t=4, j=2)
                                 [j, :, :, NW * s:NW * s + NW]).then_inc(x_loaded[s], 16)

            def rows(v):
                return v.rearrange("o (r p) -> (o r) p", p=P)

            def load_vectors():
                for q in range(2):
                    sp.dma_start(lstep[64 * q:64 * q + 64, :, :],
                                 log_step[0].rearrange("(b q g) -> q b g", q=2, g=8)[q]
                                 .partition_broadcast(64)).then_inc(step_loaded, 16)
                for k, lam in enumerate((lambda_re, lambda_im)):
                    for b in range(4):
                        r0 = 64 + 32 * k + 8 * b
                        sp.dma_start(vec_rows[r0:r0 + 8, :].rearrange("g (q p) -> g q p", q=2),
                                     lam[0, 16 * b:16 * b + 16, :]
                                     .rearrange("(q g) p -> g q p", q=2)).then_inc(rows_loaded, 16)
                for src, r0, n in ((rows(norm_mix), 0, 16), (rows(norm_ffn), 16, 16),
                                   (rows(b_glu), 32, 8),
                                   (b_pool.rearrange("o k (r p) -> (o k r) p", p=P), 40, 8),
                                   (rows(pool_scale), 48, 8),
                                   (d_skip.rearrange("o (r g) h -> (o r) (g h)", g=8), 56, 8)):
                    sp.dma_start(vec_rows[r0:r0 + n, :], src).then_inc(rows_loaded, 16)

            def load_c():
                for k, cm in enumerate((c_re, c_im)):
                    sp.dma_start(c_raw[k][:, :, :],
                                 cm[0].rearrange("(b g) h p -> (g h) b p", g=8)).then_inc(c_loaded, 16)

            def load_b(q):
                for k, bm in enumerate((b_re, b_im)):
                    for b in range(4):
                        sp.dma_start(b_raw[k][64 * q:64 * q + 64, b, :, :],
                                     bm[0, 16 * b + 8 * q:16 * b + 8 * q + 8, :, :]
                                     .rearrange("g p h -> p g h")).then_inc(b_loaded, 16)

            for s in range(4):
                load_x(s)
                if s < RAW_SLOTS:
                    load(s, static_src(s))
            load_vectors()

            def store_u(r):
                wait_emptied(sp, f"in{r // 2}")
                sp.dma_start(u_dram[2 * r:2 * r + 2].rearrange("b p k c -> p b k c"),
                             UG[:, 2 * r:2 * r + 2, :, :]).then_inc(u_stored, 16)

            def load_u8(r):
                sp.wait_ge(u_stored, 32 * (r // 2 + 1))
                if r:
                    wait_aux(sp, f"e{r - 1}")
                for d in range(CH):
                    sp.dma_start(U8[16 * d:16 * d + 16, :, :, :],
                                 u_dram[2 * r:2 * r + 2, :, CH - 1 - d, :]
                                 .rearrange("q (g h) c -> h q g c", h=GCH)).then_inc(u8_loaded, 16)

            store_at = {13: (0, 1), 21: (2, 3)}
            u8_at = {13: 0, 17: 1, 23: 2, 29: 3}
            for n in range(RAW_SLOTS, P_LOOP):
                load(n, static_src(n))
                if n == 3:
                    load_c()
                if n in (4, 5):
                    load_b(n - 4)
                for r in store_at.get(n, ()):
                    store_u(r)
                if n in u8_at:
                    load_u8(u8_at[n])
                if P_OUT + 6 <= n < P_OUT + 10:
                    if n == P_OUT + 6:
                        sp.wait_ge(ms_rdy, 8)
                        sp.wait_ge(pool_rdy, 8)
                    load_x(n - (P_OUT + 6))

            with nc.sync.Fori(0, FG - 1) as i:
                for m in range(PER):
                    if m < 8:
                        src = w_gate[0, 256 * m:256 * m + 256, bass.ds(i * NW + NW, NW)]
                    elif m < 16:
                        c, kp = divmod(m - 8, 2)
                        src = w_down[0, bass.ds(i * NW + 256 * kp, 256), c * NW:(c + 1) * NW]
                    else:
                        src = w_up[0, 256 * (m - 16):256 * (m - 16) + 256, bass.ds(i * NW + NW, NW)]
                    load(P_LOOP + m, src.rearrange("(k p) n -> p k n", p=P),
                         done=i * PER + (P_LOOP + m - RAW_SLOTS + 1))
            for kp in range(2):
                for c in range(4):
                    load(P_LAST + late_place(c, kp),
                         pair_src(w_down, (FG - 1) * NW + 256 * kp, slice(c * NW, (c + 1) * NW)))
            sp.dma_start(gfin[:, :], norm_final.partition_broadcast(P)).then_inc(gf_loaded, 16)
            for t in range(4):
                for part in range(2):
                    cs = slice(2 * NW * part, 2 * NW * (part + 1))
                    sp.wait_ge(o_rdy, 2 * t + part + 1)
                    for j in range(2):
                        sp.dma_start(out[0, 2 * t + j:SEQ:CH, cs], res_tok[64 * j:64 * j + 64, t, cs]) \
                            .then_inc(out_stored, 16)
            sp.wait_ge(out_stored, 16 * 16)

        @block.scalar
        def _(act):
            def round_hi(n, full=None, used=None):
                act.wait_ge(raw_full[n % RAW_SLOTS], 16 * (n // RAW_SLOTS + 1) if full is None else full)
                used = slot_used(n) if used is None else used
                if used is not None:
                    act.wait_ge(w_used, used)
                nc.scalar.copy(split_slot(n)[0][:, :, :], raw[n % RAW_SLOTS][:, :, :]).then_inc(hi_done, 1)

            def h_tiles(kind, s):
                wait_aux(act, f"{kind}{s}")
                half = jobs[f"{kind}{s}"][0]
                for b in range(4):
                    k, tile = h_tile(kind, s, b)
                    nc.scalar.activation(H_hi[:, tile, :], ps[:, half, b, :], ACT.Copy,
                                         scale=vecs[:, k:k + 1]).then_inc(h_hi, 1)

            def square(t, rows_=x_tok, before=0):
                if before + t:
                    act.wait_ge(row_sq, before + t)
                nc.scalar.activation(sq_junk[:, :], rows_[:, t, :], ACT.Square,
                                     accum_out=ssq[:, t, 0:1]).then_inc(row_sq, 1)

            act.dma_start(gain_rows[:, :], norm_mix.rearrange("o (r p) -> (o r) p", p=P)) \
                .then_inc(gains_loaded, 16)
            round_hi(0)
            wait_emptied(act, "gains")
            h_tiles("xt", 0)
            round_hi(1)
            h_tiles("xt", 1)
            round_hi(2)
            for s in range(4):
                act.wait_ge(x_loaded[s], 32)
            square(0)
            square(1)
            round_hi(3)
            square(2)
            square(3)
            h_tiles("xt", 2)
            round_hi(4)
            act.wait_ge(trig_in, 1)
            nc.scalar.activation(par[:, 8, :], par[:, 6, :], ACT.Sin).then_inc(trig, 1)
            nc.scalar.activation(par[:, 9, :], par[:, 7, :], ACT.Sin).then_inc(trig, 1)
            act.wait_ge(var_rdy, 1)
            nc.scalar.activation(stok[:, :], vtok[:, :], ACT.Sqrt).then_inc(root_done, 1)
            round_hi(5)
            h_tiles("xt", 3)

            def small(kind, r):
                half = jobs[key(kind, r)][0]
                if kind == "a":
                    wait_aux(act, f"a{r}")
                    for b in range(4):
                        last = nc.scalar.copy(
                            QT[:, b // 2, 4 * (b % 2):4 * (b % 2) + 4, :],
                            ps[:, half, b, :].rearrange("p (g q) -> p g q", g=4))
                    last.then_inc(free[half], 1)
                elif kind == "e":
                    wait_aux(act, f"e{r}")
                    act.wait_ge(s_cleared, 2)
                    if r:
                        act.wait_ge(s_rdy, r)
                    for k, st in enumerate((s_re, s_im)):
                        last = nc.scalar.copy(st[:, :, 1:],
                                              ps[:, half, k, :].rearrange("p (g c) -> p g c", g=8))
                    last.then_inc(free[half], 1)
                elif kind == "i":
                    wait_aux(act, f"i{r}")
                    for q in range(2):
                        last = nc.scalar.copy(
                            yt[:, :, q, :].rearrange("c i (g h) -> c g i h", h=GCH),
                            ps[:, half, q, :].rearrange("c (g i h) -> c g i h", g=8, h=GCH))
                    last.then_inc(free[half], 1)
                elif kind == "y":
                    wait_aux(act, f"y{r}")
                    for q in range(2):
                        last = nc.scalar.activation(
                            UG[:, 2 * r + q, :, :], ps[:, half, q, :].rearrange("p (j c) -> p j c", j=CH),
                            ACT.Gelu)
                    last.then_inc(free[half], 1)
                elif kind == "rt":
                    h_tiles("rt", r)

            for n in range(6, P_LOOP):
                round_hi(n)
                behind = n - SPLIT_SLOTS
                for kind, r in after.get(behind, []):
                    small(kind, r)
                for s in range(2):
                    if behind == P_GLU + 4 * s + 3:
                        act.wait_ge(w_used, behind + 1)
                        half = jobs[f"gl{s}"][0]
                        if s:
                            act.wait_ge(ms_rdy, 4)
                        for b in range(4):
                            last = nc.scalar.activation(gsig[:, b, :], ps[:, half, b, :], ACT.Sigmoid,
                                                        bias=vecs[:, 32 + 4 * s + b:33 + 4 * s + b])
                        last.then_inc(free[half], 1)
                if P_GATE <= behind < P_GATE + 4:
                    wait_emptied(act, "wo3")
                    square(behind - P_GATE, res_tok, 4)
                if behind == P_GATE + 4:
                    act.wait_ge(var_rdy, 2)
                    nc.scalar.activation(stok[:, :], vtok[:, :], ACT.Sqrt).then_inc(root_done, 1)
                if behind == P_GATE + 7:
                    wait_emptied(act, "gate")
                    for b in range(4):
                        nc.scalar.activation(gate[:, b, :], gate[:, b, :], ACT.Silu).then_inc(silu_done, 1)

            with nc.scalar.Fori(0, FG - 1) as i:
                for m in range(PER):
                    n = P_LOOP + m
                    round_hi(n, full=i * (16 * PER // RAW_SLOTS) + 16 * (n // RAW_SLOTS + 1),
                             used=i * PER + (n - SPLIT_SLOTS + 1))
                    if m == 7 + SPLIT_SLOTS:
                        act.wait_ge(*loop_free("gate", i, 1))
                        for b in range(4):
                            nc.scalar.activation(gate[:, b, :], gate[:, b, :], ACT.Silu) \
                                .then_inc(silu_done, 1)
            for m in range(8):
                round_hi(P_LAST + m)
            for t in range(4):
                for c in range(4):
                    m = 4 * t + c
                    act.wait_ge(fin_rdy, m + 1)
                    if m:
                        act.wait_ge(fin_sq, m)
                    nc.scalar.activation(fsq[:, :], res_tok[:, t, NW * c:NW * c + NW], ACT.Square,
                                         accum_out=ssq[:, t, c:c + 1]).then_inc(fin_sq, 1)
                act.wait_ge(var_rdy, 3 + t)
                nc.scalar.activation(stok[:, t:t + 1], vtok[:, t:t + 1], ACT.Sqrt).then_inc(root_done, 1)

        @block.gpsimd
        def _(gp):
            nc.gpsimd.memset(ident[:, :], 0.0).then_inc(consts, 1)
            nc.gpsimd.memset(ones[:, :], 1.0).then_inc(consts, 1)
            nc.gpsimd.memset(mask[:, :, :], 1.0).then_inc(consts, 1)
            gp.wait_ge(consts, 3)
            nc.gpsimd.affine_select(out=ident[:, :], in_=ident[:, :], compare_op=ALU.not_equal, fill=1.0,
                                    base=0, pattern=[[-1, P]], channel_multiplier=1).then_inc(consts, 1)
            nc.gpsimd.affine_select(out=mask[:, :, :], in_=mask[:, :, :], compare_op=ALU.is_ge, fill=0.0,
                                    base=0, pattern=[[-GCH, 8], [0, GCH]], channel_multiplier=1) \
                .then_inc(consts, 1)
            gp.wait_ge(consts, 5)
            nc.gpsimd.affine_select(out=mask[:, :, :], in_=mask[:, :, :], compare_op=ALU.is_ge, fill=0.0,
                                    base=GCH - 1, pattern=[[GCH, 8], [0, GCH]], channel_multiplier=-1) \
                .then_inc(consts, 1)
            for c in range(2):
                for j in range(CH):
                    nc.gpsimd.memset(inv_n[:, c, j:j + 1], 1.0 / (CH * c + j + 1)).then_inc(consts, 1)
            ALL_CONSTS = 6 + 2 * CH

            def rest_lo(n, done=None):
                gp.wait_ge(hi_done, n + 1 if done is None else done)
                hi, lo = split_slot(n)
                nc.gpsimd.tensor_tensor(lo[:, :, :], raw[n % RAW_SLOTS][:, :, :],
                                        hi[:, :, :].bitcast(f32), sub).then_inc(lo_done, 1)

            steps = [0]

            def step(ins):
                steps[0] += 1
                ins.then_inc(gp_chain, 1)

            def settle():
                gp.wait_ge(gp_chain, steps[0])

            pieces = [(k, level) for k in range(4, 8) for level in range(levels(k) + 1)]
            gp.wait_ge(consts, ALL_CONSTS)
            for n in range(P_LOOP):
                rest_lo(n)
                if n < 26:
                    continue
                if n == 26:
                    wait_emptied(gp, "in2")
                for k, level in pieces[:2]:
                    pieces.pop(0)
                    if level < levels(k):
                        shifted_add(nc.gpsimd, step, settle, pl, k, level)
                    else:
                        window_mean(nc.gpsimd, step, settle, pl, pl_s, k).then_inc(pooled, 1)
                        gp.wait_ge(pooled, k - 3)
                        break
            with nc.gpsimd.Fori(0, FG - 1) as i:
                for m in range(PER):
                    rest_lo(P_LOOP + m, i * PER + (P_LOOP + m + 1))
            for m in range(8):
                rest_lo(P_LAST + m)

        @block.vector
        def _(dve):
            steps = [0]

            def step(ins):
                steps[0] += 1
                ins.then_inc(chain, 1)

            def settle():
                dve.wait_ge(chain, steps[0])

            def tt(o, a, b, op):
                step(nc.vector.tensor_tensor(o, a, b, op))

            def ts(o, a, s1, s2, op0, op1=None):
                if op1 is None:
                    step(nc.vector.tensor_scalar(o, a, s1, None, op0))
                else:
                    step(nc.vector.tensor_scalar(o, a, s1, s2, op0, op1))

            def stt(o, a, s, b, op0, op1):
                step(nc.vector.scalar_tensor_tensor(out=o, in0=a, scalar=s, in1=b, op0=op0, op1=op1))

            def inverse_root(y, var, root, nth):
                dve.wait_ge(root_done, nth)
                step(nc.vector.reciprocal(y, root))
                settle()
                tt(root, y, y, mult)
                settle()
                tt(root, root, var, mult)
                settle()
                ts(root, root, -0.5, 1.5, mult, add)
                settle()
                tt(y, y, root, mult)
                settle()

            wait_aux(dve, "gains")
            half = jobs["gains"][0]
            nc.vector.tensor_copy(vecs[:, 0:KT], ps[:, half, 0, 0:KT]).then_inc(free[half], 1)
            wait_emptied(dve, "gains")

            def h_tiles(kind, s):
                wait_aux(dve, f"{kind}{s}")
                half = jobs[f"{kind}{s}"][0]
                for b in range(4):
                    k, tile = h_tile(kind, s, b)
                    dve.wait_ge(h_hi, k + 1)
                    last = nc.vector.scalar_tensor_tensor(
                        out=H_lo[:, tile, :], in0=ps[:, half, b, :], scalar=vecs[:, k:k + 1],
                        in1=H_hi[:, tile, :].bitcast(f32), op0=mult, op1=sub)
                    if b == 1:
                        last.then_inc(h_lo, 1)
                last.then_inc(free[half], 1)

            def spread_rms(nth):
                inverse_root(rtok[:, :], vtok[:, :], stok[:, :], nth)
                for t in range(4):
                    nc.vector.tensor_scalar(diag[:, t, :], ident[:, :], rtok[:, t:t + 1], None, mult) \
                        .then_inc(diag_rdy, 1)

            def mean_square(nth):
                dve.wait_ge(row_sq, 4 * nth)
                nc.vector.tensor_scalar(vtok[:, :], ssq[:, :, 0], 1.0 / D_MODEL, EPS, mult, add) \
                    .then_inc(var_rdy, 1)

            def take_rstd(name):
                wait_aux(dve, name)
                half = jobs[name][0]
                nc.vector.tensor_copy(rstd[:, :], ps[:, half, 0, :]).then_inc(free[half], 1)
                wait_emptied(dve, name)
            h_tiles("xt", 0)
            h_tiles("xt", 1)
            wait_aux(dve, "vec")
            half = jobs["vec"][0]
            nc.vector.tensor_copy(vecs[:, KT:P], ps[:, half, 0, KT:P]).then_inc(free[half], 1)
            wait_emptied(dve, "vec")

            lr, li = vecs[:, 64:96], vecs[:, 96:128]
            v_ = [par[:, k, :] for k in range(22)]
            LOG2E, MAGIC = 1.0 / math.log(2.0), 1.5 * 2.0 ** 23
            LN2_HI = 0.693145751953125
            LN2_LO = math.log(2.0) - LN2_HI

            def exp_parts(src, two_n, f, em1):
                ts(f, src, -88.0, 88.0, ALU.max, ALU.min)
                settle()
                ts(two_n, f, LOG2E, MAGIC, mult, add)
                settle()
                ts(two_n, two_n, MAGIC, None, sub)
                settle()
                stt(f, two_n, -LN2_HI, f, mult, add)
                settle()
                stt(f, two_n, -LN2_LO, f, mult, add)
                settle()
                ts(em1, f, 1.0 / 5040, None, mult)
                for c in (720, 120, 24, 6, 2, 1):
                    settle()
                    stt(em1, em1, 1.0 / c, f, add, mult)
                ts(pari[:, :], two_n, 127.0, 2.0 ** 23, add, mult)
                settle()
                step(nc.vector.tensor_copy(two_n, pari[:, :].bitcast(f32)))
                settle()

            dve.wait_ge(step_loaded, 32)
            exp_parts(lstep[:, :, :].rearrange("p b g -> p (b g)"), v_[0], v_[1], v_[2])
            tt(v_[3], v_[2], v_[0], mult)
            settle()
            tt(v_[3], v_[3], v_[0], add)
            settle()
            tt(v_[4], lr, v_[3], mult)
            tt(v_[5], li, v_[3], mult)
            settle()
            ts(v_[0], v_[5], 1.0 / (2 * math.pi), MAGIC, mult, add)
            settle()
            ts(v_[0], v_[0], MAGIC, None, sub)
            settle()
            c1, c2 = 6.28125, 0.00193500518798828125
            for c in (c1, c2, 2 * math.pi - c1 - c2):
                stt(v_[5], v_[0], -c, v_[5], mult, add)
                settle()
            ts(v_[6], v_[5], 0.5, None, mult)
            settle()
            ts(v_[6], v_[6], -math.pi / 2, math.pi / 2, ALU.max, ALU.min)
            settle()
            ts(v_[7], v_[6], -1.0, None, mult)
            settle()
            tt(v_[7], v_[7], v_[6], ALU.min)
            settle()
            nc.vector.tensor_scalar(v_[7], v_[7], math.pi / 2, None, add).then_inc(trig_in, 1)
            mean_square(1)
            h_tiles("xt", 2)
            exp_parts(v_[4], v_[0], v_[1], v_[2])
            dve.wait_ge(consts, 6)
            spread_rms(1)
            h_tiles("xt", 3)
            wait_aux(dve, "ct")
            half = jobs["ct"][0]
            step(nc.vector.tensor_copy(ct_re[:, :, :, :].rearrange("p b g h -> p (b g h)"),
                                       ps[:, half, 0, :]))
            nc.vector.tensor_scalar(ct_in[:, :, :, :].rearrange("p b g h -> p (b g h)"),
                                    ps[:, half, 1, :], -1.0, None, mult).then_inc(free[half], 1)
            wait_emptied(dve, "ct")
            tt(v_[11], v_[2], v_[0], mult)
            settle()
            tt(v_[10], v_[11], v_[0], add)
            stt(v_[11], v_[0], -1.0, v_[11], add, add)
            dve.wait_ge(trig, 2)
            tt(v_[12], v_[8], v_[9], mult)
            tt(v_[13], v_[8], v_[8], mult)
            settle()
            ts(v_[12], v_[12], 2.0, None, mult)
            ts(v_[14], v_[13], -2.0, 1.0, mult, add)
            settle()
            ts(v_[13], v_[13], -2.0, None, mult)
            step(nc.vector.memset(lp_re[:, 0, :], 1.0))
            step(nc.vector.memset(lp_im[:, 0, :], 0.0))
            tt(lp_re[:, 1, :], v_[10], v_[14], mult)
            tt(lp_im[:, 1, :], v_[10], v_[12], mult)
            tt(v_[15], v_[11], v_[14], mult)
            tt(v_[16], lr, lr, mult)
            tt(v_[17], li, li, mult)
            settle()
            tt(v_[15], v_[15], v_[13], add)
            tt(v_[16], v_[16], v_[17], add)
            settle()
            step(nc.vector.reciprocal(v_[21], v_[16]))
            tt(v_[17], v_[15], lr, mult)
            tt(v_[18], lp_im[:, 1, :], li, mult)
            tt(v_[19], lp_im[:, 1, :], lr, mult)
            tt(v_[20], v_[15], li, mult)
            settle()
            tt(v_[17], v_[17], v_[18], add)
            tt(v_[19], v_[19], v_[20], sub)
            settle()
            tt(v_[17], v_[17], v_[21], mult)
            tt(v_[19], v_[19], v_[21], mult)
            settle()

            def cmul(o, a, b, t1, t2):
                tt(o[0], a[0], b[0], mult)
                tt(t1, a[1], b[1], mult)
                tt(o[1], a[0], b[1], mult)
                tt(t2, a[1], b[0], mult)
                settle()
                tt(o[0], o[0], t1, sub)
                tt(o[1], o[1], t2, add)
                settle()

            def cols(v, n):
                return v.unsqueeze(2).to_broadcast([P, 32, n])

            def by_state(t):
                return t[:, :, :, :].rearrange("p b g h -> p (b g) h")

            dve.wait_ge(b_loaded, 16 * 16)
            cmul((by_state(bb_re), by_state(bb_im)), (cols(v_[17], GCH), cols(v_[19], GCH)),
                 (by_state(b_raw[0]), by_state(b_raw[1])), t512[0][:, :, :], t512[1][:, :, :])
            for first, n, by in ((2, 1, 1), (3, 2, 2), (5, 4, 4)):
                fac = [t[:, by, :].unsqueeze(1).to_broadcast([P, n, 32]) for t in (lp_re, lp_im)]
                cmul((lp_re[:, first:first + n, :], lp_im[:, first:first + n, :]),
                     (lp_re[:, 1:1 + n, :], lp_im[:, 1:1 + n, :]), fac,
                     pw[0][:, 0:n, :], pw[1][:, 0:n, :])

            take_rstd("rms")

            shape4 = [P, 8, CH, GCH]
            tmp = tmp1024[:, :, :, :]
            Q_re, Q_im = QR[0][:, :, :, :], QR[1][:, :, :, :]

            def power(t, first, r):
                return t[:, first:first + CH, 8 * r:8 * r + 8].rearrange("p d g -> p g d") \
                    .unsqueeze(3).to_broadcast(shape4)

            def chan(t, r):
                return t[:, r, :, :].unsqueeze(2).to_broadcast(shape4)

            def build_q(r):
                if r:
                    wait_aux(dve, f"i{r - 1}")
                tt(Q_re, power(lp_re, 0, r), chan(bb_re, r), mult)
                tt(tmp, power(lp_im, 0, r), chan(bb_im, r), mult)
                settle()
                tt(Q_re, Q_re, tmp, sub)
                tt(Q_im, power(lp_re, 0, r), chan(bb_im, r), mult)
                settle()
                tt(tmp, power(lp_im, 0, r), chan(bb_re, r), mult)
                settle()
                nc.vector.tensor_tensor(Q_im, Q_im, tmp, add).then_inc(q_rdy, 1)
                dve.wait_ge(q_rdy, r + 1)
                if r:
                    wait_aux(dve, f"y{r - 1}")
                for k in range(2):
                    nc.vector.tensor_copy(Q2[k][:, :, :, :].rearrange("p d g h -> p g d h"),
                                          QR[k][:, :, :, :]).then_inc(q2_rdy, 1)

            def build_r(r):
                wait_aux(dve, f"b{r}")
                tt(Q_re, power(lp_re, 1, r), chan(ct_re, r), mult)
                tt(tmp, power(lp_im, 1, r), chan(ct_in, r), mult)
                settle()
                tt(Q_re, Q_re, tmp, add)
                tt(Q_im, power(lp_re, 1, r), chan(ct_in, r), mult)
                settle()
                tt(tmp, power(lp_im, 1, r), chan(ct_re, r), mult)
                settle()
                nc.vector.tensor_tensor(Q_im, Q_im, tmp, sub).then_inc(r_rdy, 1)
                dve.wait_ge(r_rdy, r + 1)

            def taps(r):
                wait_aux(dve, f"b{r}")
                half = jobs[f"b{r}"][0]
                mk = mask[:, :, :].rearrange("p g h -> p (g h)").unsqueeze(1).to_broadcast([P, 4, P])
                for b in range(4):
                    ins = nc.vector.tensor_tensor(
                        BD[:, b // 2, 4 * (b % 2):4 * (b % 2) + 4, :],
                        ps[:, half, b, :].rearrange("p (d m) -> p d m", d=4), mk, mult)
                    if b < 3:
                        step(ins)
                ins.then_inc(free[half], 1)
                settle()
                for q in range(2):
                    k = 56 + 2 * r + q
                    nc.vector.scalar_tensor_tensor(out=BD[:, q, 0, :], in0=ident[:, :],
                                                   scalar=vecs[:, k:k + 1], in1=BD[:, q, 0, :],
                                                   op0=mult, op1=add).then_inc(bd_rdy, 1)

            def states(r):
                wait_emptied(dve, f"e{r}")
                pc, pn = ph_c[:, 8 * r:8 * r + 8, :], ph_s[:, 8 * r:8 * r + 8, :]
                ZR, ZI, ZT = zr[:, :, :], zi[:, :, :], zt[:, :, :]
                S_re, S_im = s_re[:, :, 1:], s_im[:, :, 1:]
                tt(ZR, S_re, pc, mult)
                tt(ZT, S_im, pn, mult)
                settle()
                tt(ZR, ZR, ZT, add)
                tt(ZI, S_im, pc, mult)
                settle()
                tt(ZT, S_re, pn, mult)
                settle()
                tt(ZI, ZI, ZT, sub)
                settle()
                for z in (zr, zi):
                    for g in range(8):
                        rho = v_[10][:, 8 * r + g:8 * r + g + 1].to_broadcast([P, NC])
                        step(nc.vector.tensor_tensor_scan(z[:, g, :], rho, z[:, g, :], 0.0, mult, add))
                settle()
                tt(S_re, ZR, pc, mult)
                tt(ZT, ZI, pn, mult)
                settle()
                tt(S_re, S_re, ZT, sub)
                tt(S_im, ZI, pc, mult)
                settle()
                tt(ZT, ZR, pn, mult)
                settle()
                nc.vector.tensor_tensor(S_im, S_im, ZT, add).then_inc(s_rdy, 1)
                dve.wait_ge(s_rdy, r + 1)

            def small(kind, r):
                if kind == "a" and r == ROUNDS - 1:
                    for k in range(4):
                        split_g(k)
                elif kind == "b":
                    taps(r)
                elif kind == "e":
                    build_r(r)
                    states(r)
                    if r == 0:
                        double_table(NC // 2, 8, 32)
                elif kind == "i" and r + 1 < ROUNDS:
                    build_q(r + 1)

            def split_tile(src, hi, lo, done):
                step(nc.vector.tensor_copy(hi, src))
                settle()
                nc.vector.tensor_tensor(lo, src, hi.bitcast(f32), sub).then_inc(done, 1)

            def projection(s):
                dve.wait_ge(w_used, 8 * s + 8)
                half, first = jobs[f"in{s}"][0], 4 * IN_COLS[s]
                for b in range(4):
                    dst = (UG, V)[first // 8][:, first % 8 + b, :, :]
                    ins = nc.vector.tensor_tensor(
                        dst, ps[:, half, b, :].rearrange("p (j c) -> p j c", j=CH),
                        rstd[:, :].rearrange("p (j c) -> p j c", j=CH), mult)
                ins.then_inc(free[half], 1)

            def split_g(k):
                wait_emptied(dve, f"y{k // 2}")
                dve.wait_ge(w_used, 24 + k // 2 + 1)
                split_tile(UG[:, k, :, :].rearrange("p j c -> p (j c)"), H_hi[:, k, :], H_lo[:, k, :],
                           g_rdy)

            def split_pooled(k):
                split_tile(V[:, k, :, :].rearrange("p j c -> p (j c)"), H_hi[:, 8 + k, :],
                           H_lo[:, 8 + k, :], pool_rdy)

            build_q(0)
            projection(0)
            def square_phase():
                tt(v_[0], v_[14], v_[14], mult)
                tt(v_[1], v_[12], v_[12], mult)
                tt(v_[2], v_[14], v_[12], mult)
                settle()
                tt(v_[14], v_[0], v_[1], sub)
                ts(v_[12], v_[2], 2.0, None, mult)
                settle()

            for _ in range(3):
                tt(v_[10], v_[10], v_[10], mult)
                square_phase()
            step(nc.vector.memset(ph_c[:, :, 0:1], 1.0))
            step(nc.vector.memset(ph_s[:, :, 0:1], 0.0))
            settle()
            def double_table(n, first, last):
                cs = slice(first, last)
                w_c, w_s = (v[:, cs].unsqueeze(2).to_broadcast([P, last - first, n])
                            for v in (v_[14], v_[12]))
                cmul((ph_c[:, cs, n:2 * n], ph_s[:, cs, n:2 * n]), (ph_c[:, cs, 0:n], ph_s[:, cs, 0:n]),
                     (w_c, w_s), pt[0][:, cs, 0:n], pt[1][:, cs, 0:n])

            n = 1
            while n < NC // 2:
                double_table(n, 0, 32)
                n *= 2
                square_phase()
            double_table(NC // 2, 0, 8)
            nc.vector.memset(s_re[:, :, 0:1], 0.0).then_inc(s_cleared, 1)
            nc.vector.memset(s_im[:, :, 0:1], 0.0).then_inc(s_cleared, 1)

            for pair in range(9, P_GLU):
                if pair % 8 == 7:
                    projection(pair // 8)
                if pair == P_GLU - 1:
                    for k in range(4, 6):
                        split_g(k)
                for kind, r in after.get(pair, []):
                    small(kind, r)

            wait_emptied(dve, "in3")
            dve.wait_ge(consts, 6 + 2 * CH)
            for k in range(4):
                for level in range(levels(k)):
                    shifted_add(nc.vector, step, settle, dpl, k, level)
                step(window_mean(nc.vector, step, settle, dpl, dpl_s, k))
                settle()
                split_pooled(k)
            for k in range(6, 8):
                split_g(k)
            def gated(s):
                wait_emptied(dve, f"gl{s}")
                for b in range(4):
                    tt(gsig[:, b, :], gsig[:, b, :],
                       UG[:, 4 * s + b, :, :].rearrange("p j c -> p (j c)"), mult)
                settle()

            def split_gated(s):
                for b in range(4):
                    split_tile(gsig[:, b, :], M_hi[:, 4 * s + b, :], M_lo[:, 4 * s + b, :], ms_rdy)

            def pool_mixed(s):
                dve.wait_ge(w_used, P_POOL + s + 1)
                half = jobs[f"po{s}"][0]
                for b in range(4):
                    k = 4 * s + b
                    ins = nc.vector.tensor_scalar(pmix[:, b, :], ps[:, half, b, :], vecs[:, 40 + k:41 + k],
                                                  vecs[:, 48 + k:49 + k], add, mult)
                ins.then_inc(free[half], 1)
                wait_emptied(dve, f"po{s}")

            def split_pool_mixed(s):
                for b in range(4):
                    split_tile(pmix[:, b, :], H_hi[:, 4 * s + b, :], H_lo[:, 4 * s + b, :], mp_rdy)

            gated(0)
            split_gated(0)
            for k in range(4, 8):
                dve.wait_ge(pooled, k - 3)
                split_pooled(k)
            gated(1)
            pool_mixed(0)
            split_gated(1)
            split_pool_mixed(0)
            dve.wait_ge(mp_rdy, 4)
            pool_mixed(1)
            split_pool_mixed(1)
            dve.wait_ge(mp_rdy, 8)

            for s in range(4):
                dve.wait_ge(w_used, P_OUT + 8 * s + 8)
                dve.wait_ge(x_loaded[s], 64)
                half = jobs[f"wo{s}"][0]
                for t in range(4):
                    cell = (slice(None), t, slice(NW * s, NW * s + NW))
                    ins = nc.vector.tensor_tensor(res_tok[cell], ps[:, half, t, :], x_tok[cell], add)
                ins.then_inc(free[half], 1)
                h_tiles("rt", s)
            mean_square(2)
            spread_rms(2)
            take_rstd("rms2")

            def gate_out(half, used):
                dve.wait_ge(w_used, used)
                for b in range(4):
                    ins = nc.vector.tensor_tensor(gate[:, b, :], ps[:, half, b, :], rstd[:, :], mult)
                ins.then_inc(free[half], 1)

            def gate_scale(first):
                for b in range(4):
                    dve.wait_ge(silu_done, first + b)
                    nc.vector.tensor_tensor(gate[:, b, :], gate[:, b, :], rstd[:, :], mult) \
                        .then_inc(scaled_rdy, 1)

            def up_out(half, used, scaled, freed, ff, new):
                dve.wait_ge(scaled_rdy, scaled)
                for b0 in (0, 2):
                    dve.wait_ge(*((up_half, new) if b0 == 0 else (w_used, used)))
                    for b in (b0, b0 + 1):
                        ins = nc.vector.tensor_tensor(gate[:, b, :], ps[:, half, b, :], gate[:, b, :],
                                                      mult)
                    if b0 == 0:
                        ins.then_inc(ff_new, 1)
                        dve.wait_ge(ff_new, new)
                    else:
                        ins.then_inc(free[half], 1)
                        dve.wait_ge(*freed)
                    for b in (b0, b0 + 1):
                        nc.vector.tensor_copy(F_hi[:, b, :], gate[:, b, :]).then_inc(ff_hi, 1)
                    for b in (b0, b0 + 1):
                        dve.wait_ge(ff_hi, ff + b)
                        nc.vector.tensor_tensor(F_lo[:, b, :], gate[:, b, :],
                                                F_hi[:, b, :].bitcast(f32), sub).then_inc(ff_rdy, 1)

            gate_out(jobs["gate"][0], P_UP)
            gate_scale(1)
            half, _, then = jobs["up"]
            up_out(half, P_LOOP, 4, (free[half], then), 1, 1)
            with nc.vector.Fori(0, FG - 1) as i:
                dve.wait_ge(ff_rdy, i * 4 + 4)
                gate_out(LOOP["gate"][0], i * PER + (P_LOOP + 8))
                for c in range(4):
                    half = LOOP[f"down{c}"][0]
                    dve.wait_ge(w_used, i * PER + (P_LOOP + 8 + 2 * c + 2))
                    for t in range(4):
                        cell = res_tok[:, t, NW * c:NW * c + NW]
                        ins = nc.vector.tensor_tensor(cell, ps[:, half, t, :], cell, add)
                    ins.then_inc(free[half], 1)
                    if c == 2:
                        gate_scale(i * 4 + 5)
                up_out(LOOP["up"][0], i * PER + (P_LOOP + PER), i * 4 + 8, loop_free("up", i, 1),
                       i * 4 + 5, i + 2)
            dve.wait_ge(gf_loaded, 16)
            def gained(m):
                t, c = divmod(m, 4)
                cs = slice(NW * c, NW * c + NW)
                dve.wait_ge(fin_sq, m + 1)
                tt(res_tok[:, t, cs], res_tok[:, t, cs], gfin[:, cs], mult)

            for t in range(4):
                for c in range(4):
                    dve.wait_ge(down_done, 4 * t + c + 1)
                    cell = res_tok[:, t, NW * c:NW * c + NW]
                    nc.vector.tensor_tensor(cell, ps[:, LAST_HALF[t], c, :], cell, add).then_inc(fin_rdy, 1)
                    if c:
                        gained(4 * t + c - 1)
                dve.wait_ge(fin_sq, 4 * t + 4)
                ts_ = slice(t, t + 1)
                step(nc.vector.tensor_reduce(rtok[:, ts_], ssq[:, t, :], AX.X, add))
                settle()
                nc.vector.tensor_scalar(vtok[:, ts_], rtok[:, ts_], 1.0 / D_MODEL, EPS, mult, add) \
                    .then_inc(var_rdy, 1)
                gained(4 * t + 3)
                inverse_root(rtok[:, ts_], vtok[:, ts_], stok[:, ts_], 3 + t)
                for part in range(2):
                    cs = slice(2 * NW * part, 2 * NW * (part + 1))
                    nc.vector.tensor_scalar(res_tok[:, t, cs], res_tok[:, t, cs], rtok[:, ts_], None,
                                            mult).then_inc(o_rdy, 1)

        @block.tensor
        def _(pe):
            mm = nc.tensor.matmul

            def three(o, a, b, first, last):
                (ah, al), (bh, bl) = a, b
                for part, (a_, b_) in enumerate(((ah, bh), (ah, bl), (al, bh))):
                    ins = mm(o, a_, b_, start=first and part == 0, stop=last and part == 2)
                return ins

            def weight_pair(n, half, acts, first, last):
                wh, wl = split_slot(n)
                for kt in range(2):
                    for b in range(4):
                        cs = slice(P * b, P * b + P)
                        ins = three(ps[:, half, b, :], (wh[:, kt, cs], wl[:, kt, cs]), acts[kt],
                                    first and kt == 0, last and kt == 1)
                return ins

            def last_up_pair(n, half, acts):
                wh, wl = split_slot(n)
                for b in range(4):
                    cs = slice(P * b, P * b + P)
                    for kt in range(2):
                        ins = three(ps[:, half, b, :], (wh[:, kt, cs], wl[:, kt, cs]), acts[kt],
                                    False, kt == 1)
                    if b == 1:
                        ins.then_inc(up_half, 1)
                return ins

            def token_pair(n, half, acts, first, last):
                wh, wl = split_slot(n)
                for kt in range(2):
                    ah, al = acts[kt]
                    for t in range(4):
                        ts_ = slice(P * t, P * t + P)
                        ins = three(ps[:, half, t, :], (ah[:, ts_], al[:, ts_]),
                                    (wh[:, kt, :], wl[:, kt, :]), first and kt == 0, last and kt == 1)
                return ins

            def h_at(k):
                return H_hi[:, k, :], H_lo[:, k, :]

            def m_at(k):
                return M_hi[:, k, :], M_lo[:, k, :]

            pe.wait_ge(consts, 6)
            for _ in range(WARM):
                nc.tensor.transpose(ps[:, 1, 3, 0:P], ident[:, :], ident[:, :])
            pe.wait_ge(gains_loaded, 16)
            half = wait_half(pe, "gains")
            nc.tensor.transpose(ps[:, half, 0, 0:KT], gain_rows[:, :], ident[0:KT, 0:KT]) \
                .then_inc(aux_done, 1)

            def small(kind, r):
                half = jobs[key(kind, r)][0]
                if kind != "a" or r == 0:
                    wait_half(pe, key(kind, r))
                if kind in ("xt", "rt"):
                    if kind == "xt":
                        pe.wait_ge(x_loaded[r], 32)
                    else:
                        wait_emptied(pe, f"wo{r}")
                    rows_ = x_tok if kind == "xt" else res_tok
                    for b in range(4):
                        for t in range(4):
                            k = 4 * r + b
                            ins = nc.tensor.transpose(ps[:, half, b, P * t:P * t + P],
                                                      rows_[:, t, P * k:P * k + P], ident[:, :])
                elif kind == "vec":
                    pe.wait_ge(rows_loaded, 16 * 14)
                    ins = nc.tensor.transpose(ps[:, half, 0, 0:P], vec_rows[:, :], ident[:, :])
                elif kind == "ct":
                    pe.wait_ge(c_loaded, 32)
                    for k in range(2):
                        for b in range(4):
                            ins = nc.tensor.transpose(
                                ps[:, half, k, P * b:P * b + P],
                                c_raw[k][:, 2 * b:2 * b + 2, :].rearrange("p b s -> p (b s)"), ident[:, :])
                elif kind in ("rms", "rms2"):
                    pe.wait_ge(diag_rdy, 4 if kind == "rms" else 8)
                    ins = mm(ps[:, half, 0, :], ones[:, :], diag[:, :, :].rearrange("p t n -> p (t n)"),
                             start=True, stop=True)
                elif kind == "a":
                    pe.wait_ge(q_rdy, r + 1)
                    for k in (1, 0):
                        if k == 0 and r:
                            wait_half(pe, f"a{r}")
                        for g in range(8):
                            ins = nc.tensor.transpose(
                                ps[:, half, 2 * k + g // 4, P * (g % 4):P * (g % 4) + P],
                                QR[k][:, g, :, :].rearrange("p d h -> p (d h)"), ident[:, :])
                elif kind == "b":
                    pe.wait_ge(q2_rdy, 2 * (r + 1))
                    for d in range(CH):
                        for q in range(2):
                            rows = slice(64 * q, 64 * q + 64)
                            o = ps[:, half, 2 * q + d // 4, P * (d % 4):P * (d % 4) + P]
                            for k, c_ in enumerate((ct_re, ct_in)):
                                ins = mm(o, Q2[k][rows, d, :, :].rearrange("p g h -> p (g h)"),
                                         c_[rows, r, :, :].rearrange("p g h -> p (g h)"),
                                         start=k == 0, stop=k == 1)
                elif kind == "e":
                    wait_emptied(pe, f"a{r}")
                    pe.wait_ge(u8_loaded, 16 * CH * (r + 1))
                    for k in range(2):
                        for q in range(2):
                            rows = slice(64 * q, 64 * q + 64)
                            for g in range(8):
                                ins = mm(ps[rows, half, k, NC * g:NC * g + NC], QT[:, k, g, rows],
                                         U8[:, q, g, :], start=True, stop=True)
                elif kind == "i":
                    pe.wait_ge(s_rdy, r + 1)
                    pe.wait_ge(r_rdy, r + 1)
                    for g in range(8):
                        for q in range(2):
                            rows = slice(64 * q, 64 * q + 64)
                            for jj in range(2):
                                o = ps[64 * jj:64 * jj + 64, half, q, 64 * g:64 * g + 64] \
                                    .rearrange("c (i h) -> c i h", h=GCH)
                                for k, st in enumerate((s_re, s_im)):
                                    ins = mm(o, st[rows, g, 0:NC], QR[k][rows, g, jj:CH:2, :],
                                             start=k == 0, stop=k == 1)
                elif kind == "y":
                    wait_emptied(pe, f"i{r}")
                    pe.wait_ge(bd_rdy, 2 * (r + 1))
                    for q in range(2):
                        o = ps[:, half, q, :]
                        for d in range(CH):
                            mm(o[:, NC * d:], BD[:, q, d, :],
                               UG[:, 2 * r + q, 0:CH - d, :].rearrange("p j c -> p (j c)"),
                               start=d == 0, stop=False)
                        for i in range(CH // 2):
                            ins = mm(o[:, P * i:P * i + P], yt[:, i, q, :], ident[:, :],
                                     start=False, stop=i == CH // 2 - 1)
                ins.then_inc(aux_done, 1)

            small("xt", 0)
            for n in range(P_GLU):
                s, m = divmod(n, 8)
                half = jobs[f"in{s}"][0]
                if m == 0:
                    wait_half(pe, f"in{s}")
                if s == 0 and m % 2 == 0:
                    pe.wait_ge(h_lo, m // 2 + 1)
                elif s == 0:
                    wait_emptied(pe, f"xt{m // 2}")
                pe.wait_ge(lo_done, n + 1)
                weight_pair(n, half, (h_at(2 * m), h_at(2 * m + 1)), m == 0, m == 7).then_inc(w_used, 1)
                for kind, r in after.get(n, []):
                    small(kind, r)
            for n in range(P_GLU, P_POOL):
                s, m = divmod(n - P_GLU, 4)
                half = jobs[f"gl{s}"][0]
                if m == 0:
                    wait_half(pe, f"gl{s}")
                if s == 0:
                    pe.wait_ge(g_rdy, 2 * m + 2)
                pe.wait_ge(lo_done, n + 1)
                weight_pair(n, half, (h_at(2 * m), h_at(2 * m + 1)), m == 0, m == 3).then_inc(w_used, 1)
                for kind, r in after.get(n, []):
                    small(kind, r)
            for s in range(2):
                n = P_POOL + s
                half = wait_half(pe, f"po{s}")
                pe.wait_ge(pool_rdy, 4 * s + 4)
                pe.wait_ge(lo_done, n + 1)
                wh, wl = split_slot(n)
                for b in range(4):
                    g, mt = divmod(b, 2)
                    for kt in range(2):
                        cs = slice(256 * kt + P * mt, 256 * kt + P * mt + P)
                        ins = three(ps[:, half, b, :], (wh[:, g, cs], wl[:, g, cs]),
                                    h_at(8 + 4 * s + 2 * g + kt), kt == 0, kt == 1)
                ins.then_inc(w_used, 1)
            for n in range(P_OUT, P_GATE):
                s, place, m = out_pair(n)
                half = jobs[f"wo{s}"][0]
                if place == 0:
                    wait_half(pe, f"wo{s}")
                if s == 0:
                    pe.wait_ge(*((ms_rdy, 2 * m + 2) if m < 4 else (mp_rdy, 2 * (m - 4) + 2)))
                pe.wait_ge(lo_done, n + 1)
                at_k = m_at if m < 4 else h_at
                token_pair(n, half, (at_k(2 * (m % 4)), at_k(2 * (m % 4) + 1)), place == 0, place == 7) \
                    .then_inc(w_used, 1)
                for kind, r in after.get(n, []):
                    small(kind, r)

            def ffn_pair(n, half, m, lo=None, up=False):
                pe.wait_ge(lo_done, n + 1 if lo is None else lo)
                acts = [h_at((k + 8) % 16) for k in (2 * m, 2 * m + 1)]
                if up and m == 7:
                    last_up_pair(n, half, acts).then_inc(w_used, 1)
                else:
                    weight_pair(n, half, acts, m == 0, m == 7).then_inc(w_used, 1)

            def down_pair(n, half, kp, lo):
                pe.wait_ge(lo_done, lo)
                acts = [(F_hi[:, k, :], F_lo[:, k, :]) for k in (2 * kp, 2 * kp + 1)]
                token_pair(n, half, acts, kp == 0, kp == 1).then_inc(w_used, 1)

            half = wait_half(pe, "gate")
            for m in range(8):
                if m % 2 == 0:
                    wait_emptied(pe, f"rt{m // 2}")
                ffn_pair(P_GATE + m, half, m)
                for kind, r in after.get(P_GATE + m, []):
                    small(kind, r)
            half = wait_half(pe, "up")
            for m in range(8):
                ffn_pair(P_UP + m, half, m, up=True)
            with nc.tensor.Fori(0, FG - 1) as i:
                def lo(m):
                    return i * PER + (P_LOOP + m + 1)
                pe.wait_ge(*loop_free("gate", i, 0))
                for m in range(8):
                    ffn_pair(P_LOOP + m, LOOP["gate"][0], m, lo(m))
                pe.wait_ge(ff_rdy, i * 4 + 4)
                for c in range(4):
                    pe.wait_ge(*loop_free(f"down{c}", i, 0))
                    for kp in range(2):
                        down_pair(P_LOOP + 8 + 2 * c + kp, LOOP[f"down{c}"][0], kp, lo(8 + 2 * c + kp))
                pe.wait_ge(*loop_free("up", i, 0))
                for m in range(8):
                    ffn_pair(P_LOOP + 16 + m, LOOP["up"][0], m, lo(16 + m), up=True)
            for t in range(4):
                half, ts_ = LAST_HALF[t], slice(P * t, P * t + P)
                if t < 2:
                    pe.wait_ge(free[half], loop_uses[half] + 3 * (FG - 1))
                order = [(kp, c) for kp in range(2) for c in range(4)] if t == 0 else \
                    [(kp, c) for c in range(4) for kp in range(2)]
                for kp, c in order:
                    if t >= 2 and kp == 0:
                        pe.wait_ge(fin_rdy, 4 * (t - 2) + c + 1)
                    if t == 0:
                        if c == 0:
                            pe.wait_ge(ff_rdy, 4 * (FG - 1) + 2 * kp + 2)
                        pe.wait_ge(lo_done, P_LAST + late_place(c, kp) + 1)
                    wh, wl = split_slot(P_LAST + late_place(c, kp))
                    for kt in range(2):
                        k = 2 * kp + kt
                        ins = three(ps[:, half, c, :], (F_hi[:, k, ts_], F_lo[:, k, ts_]),
                                    (wh[:, kt, :], wl[:, kt, :]), k == 0, k == 3)
                    if kp == 1:
                        ins.then_inc(down_done, 1)


_INS = ["x", "norm_mix", "w_in", "lambda_re", "lambda_im", "log_step", "b_re", "b_im", "c_re", "c_im",
        "d_skip", "w_glu", "b_glu", "w_pool", "b_pool", "pool_scale", "w_out", "norm_ffn", "w_gate",
        "w_up", "w_down", "norm_final"]


def kernel(**inputs):
    import numpy as np
    import concourse.bacc as bacc
    from concourse import mybir as mb
    from concourse.bass_utils import run_bass_kernel_spmd

    nc = bacc.Bacc("TRN2", target_bir_lowering=False, num_devices=1)
    arrays, args = {}, []
    for name in _INS:
        a = np.ascontiguousarray(inputs[name])
        arrays[f"in_{name}"] = a
        args.append(nc.dram_tensor(f"in_{name}", a.shape, mb.dt.from_np(a.dtype), kind="ExternalInput").ap())
    args.append(nc.dram_tensor("out_0", (1, SEQ, D_MODEL), mb.dt.float32, kind="ExternalOutput").ap())
    emit(nc, *args)
    r = run_bass_kernel_spmd(nc, [arrays], core_ids=[0])
    return r.results[0]["out_0"]
```
